# Optimizing a Trainium2 kernel written in Bass

```python
import jax
import jax.numpy as jnp
from jax import lax
import numpy as np

D_MODEL = 1024
BATCH = 1
SEQ = 256
DEPTH = 2

N_A_LAYERS = DEPTH // 2
N_B_LAYERS = DEPTH - N_A_LAYERS
D_FF = 4 * D_MODEL
NORM_EPS = 1e-6
RWKV_HEAD = 64
RWKV_HEADS = D_MODEL // RWKV_HEAD
D_DECAY_LORA = 64
D_AAA_LORA = 64
D_GATE_LORA = 160
GN_EPS = 64e-5
NSA_HEADS = 16
NSA_GROUPS = 4
NSA_HPG = NSA_HEADS // NSA_GROUPS
HEAD_DIM = 64
CMP_LEN = 32
CMP_STRIDE = 16
CMP_RATIO = CMP_LEN // CMP_STRIDE
SLC_LEN = 64
SLC_RATIO = SLC_LEN // CMP_STRIDE
TOP_N = 16
WINDOW = 512
PHI_HIDDEN = 128
Q_BLOCK = 64
N_KV_SLOTS = 6
FORCED_SCORE = 1e4
NEG_INF = -1e30

kernel_name = 'hybrid_rwkv7_nsa_yoco'

def rms_norm(x, g):
    xf = x.astype(jnp.float32)
    y = xf * lax.rsqrt(jnp.mean(xf * xf, axis=-1, keepdims=True) + NORM_EPS)
    return (y * g.astype(jnp.float32)).astype(x.dtype)

def modulate(h, shift, scale):
    return h * (1 + scale[:, None, :]) + shift[:, None, :]

def masked_softmax(s, mask):
    s = jnp.where(mask, s.astype(jnp.float32), NEG_INF)
    p = jnp.exp(s - jnp.max(s, axis=-1, keepdims=True)) * mask
    return p / jnp.maximum(jnp.sum(p, axis=-1, keepdims=True), 1e-30)

def sq_relu_mlp(h, w_up, w_down):
    return jnp.square(jax.nn.relu(h @ w_up)) @ w_down

def rwkv7_time_mix(h, mu, w_r, w_k, w_v, w_o, w0, wa, wb, a0, aa, ab, ga, gb,
                   k_k, k_a, r_k, ln_g, ln_b):
    B, S, D = h.shape
    H, N = RWKV_HEADS, RWKV_HEAD
    xx = jnp.pad(h, ((0, 0), (1, 0), (0, 0)))[:, :-1] - h
    xr, xw, xk, xv, xa, xg = [h + xx * mu[i] for i in range(6)]
    r = xr @ w_r
    k = xk @ w_k
    v = xv @ w_v
    w_log = -jax.nn.softplus(-(w0 + jnp.tanh(xw @ wa) @ wb)) - 0.5
    a = jax.nn.sigmoid(a0 + (xa @ aa) @ ab)
    g = jax.nn.sigmoid(xg @ ga) @ gb

    def heads(t):
        return t.reshape(B, S, H, N).astype(jnp.float32)

    kk = heads(k * k_k)
    kk = kk / jnp.maximum(jnp.linalg.norm(kk, axis=-1, keepdims=True), 1e-12)
    k = k * (1 + (a - 1) * k_a)
    rf, kf, vf, af = heads(r), heads(k), heads(v), heads(a)
    decay = jnp.exp(-jnp.exp(heads(w_log)))

    def step(state, inp):
        r_t, d_t, k_t, v_t, kk_t, a_t = inp
        sa = jnp.einsum('bhvk,bhk->bhv', state, -kk_t)
        state = (state * d_t[:, :, None, :] + sa[..., None] * (kk_t * a_t)[:, :, None, :]
                 + v_t[..., None] * k_t[:, :, None, :])
        return state, jnp.einsum('bhvk,bhk->bhv', state, r_t)

    tm = lambda t: jnp.swapaxes(t, 0, 1)
    s0 = jnp.zeros((B, H, N, N), jnp.float32)
    _, y = lax.scan(step, s0, (tm(rf), tm(decay), tm(kf), tm(vf), tm(kk), tm(af)))
    y = tm(y)
    mean = jnp.mean(y, axis=-1, keepdims=True)
    var = jnp.mean(jnp.square(y - mean), axis=-1, keepdims=True)
    y = ((y - mean) * lax.rsqrt(var + GN_EPS)).reshape(B, S, D) * ln_g + ln_b
    bonus = jnp.sum(rf * kf * r_k, axis=-1, keepdims=True) * vf
    out = (y + bonus.reshape(B, S, D)) * g.astype(jnp.float32)
    return out.astype(h.dtype) @ w_o

def compress_blocks(tok, pos, w1, w2):
    B, S, G, Dh = tok.shape
    chunks = tok.reshape(B, S // CMP_STRIDE, CMP_STRIDE, G, Dh)
    n_cmp = S // CMP_STRIDE - CMP_RATIO + 1
    blocks = jnp.concatenate([chunks[:, r:r + n_cmp] for r in range(CMP_RATIO)], axis=2)
    blocks = blocks + pos[:, None, :]
    flat = jnp.transpose(blocks, (0, 1, 3, 2, 4)).reshape(B, n_cmp, G, CMP_LEN * Dh)
    return jax.nn.gelu(flat @ w1) @ w2

def build_shared_kv(x, c, kv_norm_g, kv_ada_w, kv_ada_b, kv_w, pos_k, pos_v,
                    k_w1, k_w2, v_w1, v_w2):
    B, S, _ = x.shape
    shift, scale = jnp.split(jax.nn.silu(c) @ kv_ada_w + kv_ada_b, 2, axis=-1)
    h = modulate(rms_norm(x, kv_norm_g), shift, scale)
    kv = (h @ kv_w).reshape(B, S, N_KV_SLOTS, NSA_GROUPS, HEAD_DIM)
    k_c, v_c, k_s, v_s, k_w, v_w = [kv[:, :, i] for i in range(N_KV_SLOTS)]
    k_cmp = compress_blocks(k_c, pos_k, k_w1, k_w2)
    v_cmp = compress_blocks(v_c, pos_v, v_w1, v_w2)
    to_blocks = lambda t: jnp.transpose(
        t.reshape(B, S // SLC_LEN, SLC_LEN, NSA_GROUPS, HEAD_DIM), (0, 3, 1, 2, 4))
    pad = ((0, 0), (WINDOW, 0), (0, 0), (0, 0))
    return (k_cmp, v_cmp, to_blocks(k_s), to_blocks(v_s), jnp.pad(k_w, pad), jnp.pad(v_w, pad))

def gather_blocks(blocks, idx):
    return jax.vmap(jax.vmap(lambda blk, ids: blk[ids]))(blocks, idx)

def nsa_attention(h, w_qg, w_o, k_cmp, v_cmp, k_slc, v_slc, k_win, v_win):
    B, S, _ = h.shape
    G, Hg, Dh, H = NSA_GROUPS, NSA_HPG, HEAD_DIM, NSA_HEADS
    qg = h @ w_qg
    q = (qg[..., :H * Dh] * Dh ** -0.5).reshape(B, S, G, Hg, Dh)
    gates = jax.nn.sigmoid(qg[..., H * Dh:].astype(jnp.float32)).reshape(B, S, G, Hg, 3)
    n_cmp = k_cmp.shape[1]
    n_slc = k_slc.shape[2]
    top_n = min(TOP_N, n_slc)
    cmp_end = jnp.arange(n_cmp) * CMP_STRIDE + CMP_LEN - 1
    blk_ids = jnp.arange(n_slc)
    offsets = [m - n + CMP_RATIO - 1 for m in range(SLC_RATIO) for n in range(CMP_RATIO)]
    pad_l = CMP_RATIO - 1
    pad_r = max(0, SLC_RATIO * (n_slc - 1) + max(offsets) + 1 - (n_cmp + pad_l))
    sel_off = jnp.arange(SLC_LEN)

    def block(i):
        t0 = i * Q_BLOCK
        t = t0 + jnp.arange(Q_BLOCK)
        qb = lax.dynamic_slice_in_dim(q, t0, Q_BLOCK, axis=1)
        gb = lax.dynamic_slice_in_dim(gates, t0, Q_BLOCK, axis=1)
        s_c = jnp.einsum('bqghd,bngd->bghqn', qb, k_cmp)
        p_c = masked_softmax(s_c, cmp_end[None, :] <= t[:, None])
        o_c = jnp.einsum('bghqn,bngd->bqghd', p_c.astype(v_cmp.dtype), v_cmp)
        imp = jnp.pad(jnp.sum(p_c, axis=2), ((0, 0), (0, 0), (0, 0), (pad_l, pad_r)))
        imp = sum(imp[..., off::SLC_RATIO][..., :n_slc] for off in offsets)
        cur = t // SLC_LEN
        forced = ((blk_ids[None] == 0) | (blk_ids[None] == cur[:, None])
                  | (blk_ids[None] == cur[:, None] - 1))
        imp = jnp.where(forced, FORCED_SCORE, imp)
        imp = jnp.where(blk_ids[None] > cur[:, None], -1.0, imp)
        _, idx = lax.top_k(imp, top_n)
        kb = gather_blocks(k_slc, idx).reshape(B, G, Q_BLOCK, top_n * SLC_LEN, Dh)
        vb = gather_blocks(v_slc, idx).reshape(B, G, Q_BLOCK, top_n * SLC_LEN, Dh)
        kpos = (idx[..., None] * SLC_LEN + sel_off).reshape(B, G, Q_BLOCK, top_n * SLC_LEN)
        s_s = jnp.einsum('bqghd,bgqkd->bghqk', qb, kb)
        p_s = masked_softmax(s_s, (kpos <= t[None, None, :, None])[:, :, None])
        o_s = jnp.einsum('bghqk,bgqkd->bqghd', p_s.astype(vb.dtype), vb)
        kw = lax.dynamic_slice_in_dim(k_win, t0, Q_BLOCK + WINDOW, axis=1)
        vw = lax.dynamic_slice_in_dim(v_win, t0, Q_BLOCK + WINDOW, axis=1)
        wpos = t0 - WINDOW + jnp.arange(Q_BLOCK + WINDOW)
        dist = t[:, None] - wpos[None, :]
        win_mask = (dist >= 0) & (dist < WINDOW) & (wpos[None, :] >= 0)
        s_w = jnp.einsum('bqghd,bkgd->bghqk', qb, kw)
        p_w = masked_softmax(s_w, win_mask)
        o_w = jnp.einsum('bghqk,bkgd->bqghd', p_w.astype(vw.dtype), vw)
        o = gb[..., 0:1] * o_c + gb[..., 1:2] * o_s + gb[..., 2:3] * o_w
        return o.astype(h.dtype)

    o = lax.map(block, jnp.arange(S // Q_BLOCK))
    o = jnp.moveaxis(o, 0, 1).reshape(B, S, H * Dh)
    return o @ w_o

def setup_inputs(seed: int = 0) -> dict:
    key = jax.random.key(seed)
    ks = iter(jax.random.split(key, 48))
    f32 = jnp.float32
    nrm = lambda shape, s: s * jax.random.normal(next(ks), shape, f32)
    D, A, Bn = D_MODEL, N_A_LAYERS, N_B_LAYERS
    GD = NSA_GROUPS * HEAD_DIM
    return {
        'x': nrm((BATCH, SEQ, D), 1.0),
        'c': nrm((BATCH, D), 1.0),
        'ada_w': nrm((DEPTH, D, 6 * D), D ** -0.5),
        'ada_b': nrm((DEPTH, 6 * D), 0.01),
        'norm_g': 1.0 + nrm((DEPTH, 4, D), 0.02),
        'mlp_up': nrm((DEPTH, D, D_FF), D ** -0.5),
        'mlp_down': nrm((DEPTH, D_FF, D), D_FF ** -0.5),
        'rw_mu': jax.random.uniform(next(ks), (A, 6, D), f32),
        'rw_r': nrm((A, D, D), D ** -0.5),
        'rw_k': nrm((A, D, D), D ** -0.5),
        'rw_v': nrm((A, D, D), D ** -0.5),
        'rw_o': nrm((A, D, D), D ** -0.5),
        'rw_w0': jnp.linspace(-6.5, -1.5, D, dtype=f32)[None] + nrm((A, D), 0.1),
        'rw_wa': nrm((A, D, D_DECAY_LORA), D ** -0.5),
        'rw_wb': nrm((A, D_DECAY_LORA, D), 0.1 * D_DECAY_LORA ** -0.5),
        'rw_a0': nrm((A, D), 0.1),
        'rw_aa': nrm((A, D, D_AAA_LORA), D ** -0.5),
        'rw_ab': nrm((A, D_AAA_LORA, D), 0.5 * D_AAA_LORA ** -0.5),
        'rw_ga': nrm((A, D, D_GATE_LORA), D ** -0.5),
        'rw_gb': nrm((A, D_GATE_LORA, D), D_GATE_LORA ** -0.5),
        'rw_kk': 0.85 + nrm((A, D), 0.05),
        'rw_ka': 1.0 + nrm((A, D), 0.05),
        'rw_rk': -0.04 + nrm((A, RWKV_HEADS, RWKV_HEAD), 0.05),
        'rw_lng': 1.0 + nrm((A, D), 0.02),
        'rw_lnb': nrm((A, D), 0.01),
        'kv_norm_g': 1.0 + nrm((D,), 0.02),
        'kv_ada_w': nrm((D, 2 * D), D ** -0.5),
        'kv_ada_b': nrm((2 * D,), 0.01),
        'kv_w': nrm((D, N_KV_SLOTS * GD), D ** -0.5),
        'cmp_pos_k': nrm((CMP_LEN, HEAD_DIM), 0.1),
        'cmp_pos_v': nrm((CMP_LEN, HEAD_DIM), 0.1),
        'cmp_k_w1': nrm((CMP_LEN * HEAD_DIM, PHI_HIDDEN), (CMP_LEN * HEAD_DIM) ** -0.5),
        'cmp_k_w2': nrm((PHI_HIDDEN, HEAD_DIM), PHI_HIDDEN ** -0.5),
        'cmp_v_w1': nrm((CMP_LEN * HEAD_DIM, PHI_HIDDEN), (CMP_LEN * HEAD_DIM) ** -0.5),
        'cmp_v_w2': nrm((PHI_HIDDEN, HEAD_DIM), PHI_HIDDEN ** -0.5),
        'nsa_wqg': nrm((Bn, D, NSA_HEADS * HEAD_DIM + 3 * NSA_HEADS), D ** -0.5),
        'nsa_wo': nrm((Bn, NSA_HEADS * HEAD_DIM, D), (NSA_HEADS * HEAD_DIM) ** -0.5),
    }

def reference(x, c, ada_w, ada_b, norm_g, mlp_up, mlp_down,
              rw_mu, rw_r, rw_k, rw_v, rw_o, rw_w0, rw_wa, rw_wb, rw_a0, rw_aa, rw_ab,
              rw_ga, rw_gb, rw_kk, rw_ka, rw_rk, rw_lng, rw_lnb,
              kv_norm_g, kv_ada_w, kv_ada_b, kv_w, cmp_pos_k, cmp_pos_v,
              cmp_k_w1, cmp_k_w2, cmp_v_w1, cmp_v_w2, nsa_wqg, nsa_wo):
    shared = None
    for layer in range(DEPTH):
        sh1, sc1, gt1, sh2, sc2, gt2 = jnp.split(
            jax.nn.silu(c) @ ada_w[layer] + ada_b[layer], 6, axis=-1)
        h = modulate(rms_norm(x, norm_g[layer, 0]), sh1, sc1)
        if layer < N_A_LAYERS:
            i = layer
            y = rwkv7_time_mix(h, rw_mu[i], rw_r[i], rw_k[i], rw_v[i], rw_o[i], rw_w0[i],
                               rw_wa[i], rw_wb[i], rw_a0[i], rw_aa[i], rw_ab[i],
                               rw_ga[i], rw_gb[i], rw_kk[i], rw_ka[i], rw_rk[i],
                               rw_lng[i], rw_lnb[i])
        else:
            if layer == N_A_LAYERS:
                shared = build_shared_kv(x, c, kv_norm_g, kv_ada_w, kv_ada_b, kv_w,
                                         cmp_pos_k, cmp_pos_v, cmp_k_w1, cmp_k_w2,
                                         cmp_v_w1, cmp_v_w2)
            j = layer - N_A_LAYERS
            y = nsa_attention(h, nsa_wqg[j], nsa_wo[j], *shared)
        x = x + gt1[:, None, :] * rms_norm(y, norm_g[layer, 1])
        h = modulate(rms_norm(x, norm_g[layer, 2]), sh2, sc2)
        y = sq_relu_mlp(h, mlp_up[layer], mlp_down[layer])
        x = x + gt2[:, None, :] * rms_norm(y, norm_g[layer, 3])
    return x


_drawn_inputs = setup_inputs


def setup_inputs(seed=0):
    import zlib

    import numpy as np

    out = dict(_drawn_inputs(seed))
    spreads = {}
    factors = {'ada_b': 2.876,
     'rw_wa': 7.181,
     'rw_wb': 6.485,
     'rw_lng': 17.577,
     'rw_lnb': 40.109,
     'kv_norm_g': 8.0,
     'kv_ada_b': 8.0,
     'cmp_pos_k': 26.731,
     'cmp_pos_v': 22.536}
    for name, (base, spread) in spreads.items():
        noise = np.random.default_rng([zlib.crc32(name.encode()), seed]).standard_normal(out[name].shape)
        drawn = base * np.exp(spread * noise) if base else spread * noise
        out[name] = jnp.asarray(drawn.astype(out[name].dtype))
    for name, factor in factors.items():
        out[name] = (out[name] * factor).astype(out[name].dtype)
    return out
```

```python
import numpy as np
import concourse.bass as bass
from concourse import mybir
from contextlib import ExitStack

F32 = mybir.dt.float32
F32R = mybir.dt.float32r
BF16 = mybir.dt.bfloat16
ALU = mybir.AluOpType
ACT = mybir.ActivationFunctionType
AX = mybir.AxisListType

P = 128
D = 1024
S = 256
DFF = 4096
KC = D // P
TB = S // P
H = 16
N = 64
NCH = S // N
G = 4
NCMP = 15
RING = 4
DECAY = float(np.exp(-0.5))
NEG = -1e30
KB = 1024


class Tally:

    def __init__(self, sem):
        self.sem, self.n, self.i, self.per = sem, 0, None, 0

    def value(self, n=None):
        n = self.n if n is None else n
        return n if self.i is None else self.i * self.per + n

    def next(self, k=1):
        self.n += k
        return self.value()

    def enter(self, i, per):
        self.i, self.per, self.start = i, per, self.n

    def leave(self, turns):
        assert self.n - self.start == self.per
        self.n += self.per * (turns - 1)
        self.i = None


class Steps:

    def __init__(self, eng, sem):
        self.eng, self.own = eng, Tally(sem)

    def do(self, ins):
        ins.then_inc(self.own.sem, 1)
        self.eng.wait_ge(self.own.sem, self.own.next())

    def tell(self, ins, tally):
        ins.then_inc(tally.sem, 1)
        self.eng.wait_ge(tally.sem, tally.next())


def scan_schedule():
    order = [(x, 0, h) for h in range(2) for x in ("prep", "turn")] + [("values", 0, 0), ("values", 0, 1), ("ada", 0, 0)]
    ada = 1
    for c in range(NCH):
        between = [(x, c - 1, 0) for x in "wusy"] if c else []
        if c + 1 < NCH:
            between += [(x, c + 1, h) for h in range(2) for x in ("prep", "turn")]
            between += [("values", c + 1, h) for h in range(2)]
        order += [("start", c, 0), ("start", c, 1)]
        for level in range(5):
            for x in "zpt"[:3 if level < 4 else 2]:
                order += [(x, c, 0, level), (x, c, 1, level)]
                if between and x != "t":
                    order.append(between.pop(0))
                elif ada < 4 * c + 4:
                    order.append(("ada", ada, 0))
                    ada += 1
        assert not between
        while ada < 4 * c + 4:
            order.append(("ada", ada, 0))
            ada += 1
        order.append(("cols", c, 2 * min(c + 2, NCH)))
    return order + [(x, NCH - 1, 0) for x in "wuy"]


def hybrid_kernel(nc, A, out):
    ctx = ExitStack()
    with ctx:
        base = 16512

        def at(name, shape, dt, kb):
            return nc.alloc_sbuf_tensor_at(name, shape, dt, offset=base + int(kb * KB))

        def sem(name):
            return ctx.enter_context(nc.semaphore(name))

        raw = [at(f"raw{i}", [P, 2048], F32, 8 * i) for i in range(RING)]
        whi = [at(f"whi{b}", [P, 4, 512], F32R, 32 + 16 * b) for b in range(2)]
        wlo = [at(f"wlo{b}", [P, 4, 512], F32R, 40 + 16 * b) for b in range(2)]
        R = 64
        hF = at("hF", [P, KC, S], F32, R)
        xxF = at("xxF", [P, KC, S], F32, R + 8)
        xm = at("xm", [P, KC, S], F32, R + 16)
        xm2 = at("xm2", [P, KC, S], F32, R + 24)
        xm3 = at("xm3", [P, KC, S], F32, R + 32)
        xhi = [at("xhi0", [P, KC, S], F32R, R + 24), at("xhi1", [P, KC, S], F32R, R + 104.5)]
        xlo = [at("xlo0", [P, KC, S], F32R, R + 32), at("xlo1", [P, KC, S], F32R, R + 112.5)]
        sgF = at("sgF", [P, KC, S], F32, R + 40)
        cumF = at("cumF", [P, KC, S], F32, R + 48)
        aF = at("aF", [P, KC, S], F32, R + 56)
        kF = at("kF", [P, KC, S], F32, R + 64)
        kkF = at("kkF", [P, KC, S], F32, R + 72)
        tmpF = at("tmpF", [P, KC, S], F32, R + 80)
        vPad = at("vPad", [P, N + KC * S + N], F32, R + 88)
        gF = at("gF", [P, KC, S], F32, R + 96.5)
        krF = at("krF", [P, NCH, KC, 2, N], F32, R + 104.5)
        bk = at("bk", [P, NCH, KC, 2, P], F32, R)
        kaF = at("kaF", [P, KC, S], F32, R + 88)
        xt = at("xt", [P, TB, D], F32, R + 80)
        junk = at("junk", [P, D], F32, R + 88)
        acc1 = at("acc1", [P, D], F32, R + 92)
        rows1 = at("rows1", [120, P], F32, R + 40)
        rows2 = at("rows2", [112, P], F32, R + 40.5)
        rows3 = at("rows3", [48, P], F32, R + 41)
        scanmask = at("scanmask", [P, KC * S], F32, R + 88)
        wa = at("wa", [P, KC, 64], F32, R + 104.5)
        aa = at("aa", [P, KC, 64], F32, R + 106.5)
        wb = at("wb", [64, D], F32, R + 108.5)
        ab = at("ab", [64, D], F32, R + 112.5)
        tw = at("tw", [64, S], F32, R + 116.5)
        ta = at("ta", [64, S], F32, R + 117.5)
        tg0 = at("tg0", [P, S], F32, R + 118.5)
        tg1 = at("tg1", [32, S], F32, R + 119.5)
        ga = at("ga", [P, KC, 160], F32, R + 64)
        gb0 = at("gb0", [P, D], F32, R + 72)
        gb1 = at("gb1", [32, D], F32, R + 76)
        acc = at("acc", [P, D], F32, 184.5)
        gt = [at(f"gt{i}", [P, D], F32, 188.5 + 4 * i) for i in range(2)]
        indt = at("indt", [H, D], F32, 196.5)
        C0 = 200.5
        ident = at("ident", [P, P], F32, C0)
        ones = at("ones", [P, P], F32, C0 + .5)
        bones = at("bones", [P, P], F32, C0 + 1)
        ind = at("ind", [P, KC, H], F32, C0 + 1.5)
        tri = at("tri", [P, 2, N], BF16, C0 + 2)
        lm = at("lm", [P, 6, P], BF16, C0 + 2.25)
        pt1 = at("pt1", [P, 120], F32, C0 + 3.75)
        pt2 = at("pt2", [P, 112], F32, C0 + 4.25)
        pt3 = at("pt3", [P, 48], F32, C0 + 4.75)
        s16 = at("s16", [H, S], F32, C0 + 5)
        vec = at("vec", [P, 192], F32, C0 + 6)
        ps = ctx.enter_context(nc.psum_tensor("ps", [P, 8, 512], F32))

        def bank(b, n=1):
            return ps[:, b:b + n, :].rearrange("p b c -> p (b c)")

        MU = {n: 8 * i for i, n in enumerate("rwkvag")}
        W0, A0, KKC, KAC, RKC, LNG, LNB, KVG, CC = range(48, 120, 8)
        NG = 0
        KVB, POSK, POSV = 64, 80, 96
        names = ["gm", "sh", "omka", "cs", "neg", "gm2", "sh2", "gmkv", "shkv"]
        V = {n: vec[:, 8 * i:8 * i + 8] for i, n in enumerate(names)}
        ss, std, rstd = (vec[:, 72 + 2 * i:74 + 2 * i] for i in range(3))
        epsc = vec[:, 78:79]
        gnepsc = vec[:, 79:80]
        PL = vec[:, 80:112].rearrange("p (c j) -> p c j", j=KC)

        s_rows = sem("rows_loaded")
        s_x = sem("x_loaded")
        s_lora = sem("lora_weights_loaded")
        s_gate_bias = sem("gate_bias_loaded")
        s_const = sem("constants_made")
        raw_in = [sem(f"raw_loaded{i}") for i in range(RING)]
        s_hi = sem("weight_high_part")
        s_lov = sem("weight_low_part_by_vector")
        s_lop = sem("weight_low_part_by_gpsimd")
        s_ws = sem("weight_parts_used")
        s_ada = sem("ada_piece_used")
        c_act, c_dve, c_pool = sem("act_step"), sem("dve_step"), sem("pool_step")
        s_pt_ps, s_pt, s_sig_c = sem("params_transposed"), sem("params_copied"), sem("sigmoid_c")
        s_xhat, s_xT, s_h = sem("xhat"), sem("xhat_transposed"), sem("h_ready")
        s_ss = sem("rms_std")
        s_rstd = sem("rms_rstd")
        s_cols_ps, s_cols = sem("ada_columns_psum"), sem("ada_columns")
        s_mix, s_mix_a = sem("mix_ready"), sem("mix_of_a_ready")
        s_l1, s_t1 = sem("lora_inner_psum"), sem("lora_inner")
        s_l2, s_t2 = sem("lora_outer_psum"), sem("lora_outer")
        s_xhi, s_xlo = sem("x_high_part"), sem("x_low_part")
        s_proj_ev = sem("projection_half_copied")
        s_cum, s_dec = sem("decay_sum"), sem("decays")
        s_kkraw, s_kksq, s_kkn_ps, s_kkstd, s_kkrs, s_kkb_ps, s_kkd = (
            sem(n) for n in ("kk_scaled", "kk_squared", "kk_norm_psum", "kk_norm", "kk_rnorm",
                             "kk_rnorm_spread_psum", "kk_normed"))
        s_kaf, s_prk, s_bonus_ps, s_bonus = sem("k_factor"), sem("r_k_product"), sem("bonus_psum"), sem("bonus")
        s_bk0, s_bk, s_kr = sem("bk_zeroed"), sem("bk_ready"), sem("kr_ready")

        def ada_pieces(w, part):
            return [("A", w[256 * i:256 * i + 256, D * part:D * part + D]
                     .rearrange("(k p) n -> p k n", p=P)) for i in range(4)]

        def w_piece(w, row, col):
            return ("W", w[row:row + 512, col:col + 512].rearrange("(k p) n -> p k n", p=P))

        def square(w):
            return [w_piece(w, 512 * kh, 512 * ch) for ch in range(2) for kh in range(2)]

        ada0, ada1 = A["ada_w"][0], A["ada_w"][1]
        start_pieces = ada_pieces(ada0, 0) + ada_pieces(ada0, 1)
        proj_pieces = (square(A["rw_k"][0]) + ada_pieces(ada0, 2) + square(A["rw_r"][0])
                       + ada_pieces(ada0, 5) + square(A["rw_v"][0]))
        scan_pieces = (ada_pieces(ada0, 3) + ada_pieces(ada0, 4) + ada_pieces(A["kv_ada_w"], 0)
                       + ada_pieces(A["kv_ada_w"], 1) + square(A["rw_o"][0]))

        stream = start_pieces + proj_pieces + scan_pieces
        W_AT = [p for p, x in enumerate(stream) if x[0] == "W"]
        A_AT = [p for p, x in enumerate(stream) if x[0] == "A"]

        def pair(name, shape, kb):
            return [at(f"{name}{i}", shape, F32, kb + 72 * i) for i in range(2)]

        knr = pair("knr", [P, KC, 2, 2, N], 32)
        qb = pair("qb", [P, KC, 2, N], 40)
        bkt = pair("bkt", [P, KC, 2, N], 44)
        uv = pair("uv", [P, KC, 2, N], 48)
        sv = pair("sv", [P, KC, 2, N], 52)
        tt = pair("tt", [P, KC, P], 56)
        xt_ = pair("xtr", [P, KC, P], 60)
        xc = at("xc", [P, KC, P], F32, R + 72)
        zs = at("zs", [P, KC, P], F32, R + 76)
        ts = at("ts", [P, KC, P], F32, R + 80)
        wc = at("wc", [P, KC, N], F32, R + 84)
        state = at("state", [P, KC, N], F32, R + 86)
        yF = at("yF", [P, KC, S], F32, R + 32)
        vF = vPad[:, N:N + KC * S].rearrange("p (j t) -> p j t", j=KC)

        by_half = lambda name: [sem(f"{name}_{h}") for h in range(2)]
        s_prep_ps, s_knr, s_bkt_ps, s_bkt = sem("prep_psum"), sem("prep_masked"), sem("bk_transposed"), sem("bk_copied")
        s_v_ps, s_v = sem("v_transposed"), sem("v_copied")
        s_krc, s_state_sv, s_zeroed = sem("kr_copied"), sem("state_copied"), sem("workspace_zeroed")
        s_tt0, s_t_ps, s_ts, s_xc, s_z_ps, s_zs, s_p_ps, s_tt = (
            by_half(n) for n in ("inverse_begun", "inverse_turned", "inverse_copied", "level_blocks",
                                 "z_psum", "z_copied", "p_psum", "inverse_raised"))
        s_w_ps, s_w, s_u_ps, s_u, s_st_ps, s_st, s_y_ps, s_y = (
            sem(n) for n in ("w_psum", "w_copied", "u_psum", "u_copied", "state_psum", "state_new",
                             "y_psum", "y_copied"))
        SCAN = scan_schedule()

        xr = at("xr", [P, TB, D], F32, R)
        xn = at("xn", [P, TB, D], F32, R + 8)
        ghi, glo = at("ghi", [P, KC, S], F32R, R + 16), at("glo", [P, KC, S], F32R, R + 24)
        hfull = at("hfull", [P, KC, S], F32, R + 32)
        sqF = at("sqF", [P, KC, S], F32, R + 8)
        zF = at("zF", [P, KC, S], F32, R + 40)
        nrow = [at("nrow0", [P, D], F32, R + 48), at("nrow1", [P, D], F32, R + 52)]
        pn = at("pn", [P, D], F32, R + 56)
        junk2 = at("junk2", [P, D], F32, R + 60)
        rs16 = at("rs16", [H, S], F32, R + 72)
        relu = at("relu", [P, 4, S], F32, R + 40)
        hid = at("hid", [P, 4, S], F32, R + 44)
        hidhi = [at(f"hidhi{i}", [P, 4, S], F32R, R + 48 + 4 * i) for i in range(2)]
        hidlo = [at(f"hidlo{i}", [P, 4, S], F32R, R + 56 + 4 * i) for i in range(2)]
        acc6 = at("acc6", [P, 6 * D], F32, R + 64)
        zero = at("zero", [P, P], BF16, C0 + 6.75)
        qT = at("qT", [P, KC, S], F32, R + 40)
        kall = at("kall", [P, G, 2, 2, S], F32, R + 48)
        vtok = at("vtok", [P, TB, 2, S], F32, R + 64)
        kcF = at("kcF", [P, 2, 2, S], F32, R + 68)
        stk = at("stk", [P, 2, G, S], F32, R + 76)
        nrow_b = [at("nrow2", [P, D], F32, R + 88), at("nrow3", [P, D], F32, R + 92)]
        xcmp = at("xcmp", [P, 2, 16, 64], F32, R + 88)
        w1 = [at(f"cmpw1{i}", [P, 16, P], F32, R + 96 + 8 * i) for i in range(2)]
        qhi, qlo = at("qhi", [P, KC, S], F32R, R + 8), at("qlo", [P, KC, S], F32R, R + 112)
        gB = [at("gateB0", [P, D], F32, R + 72), at("gateB1", [P, D], F32, 192.5)]
        prob = [at(f"prob{i}", [P, 2, 2, S], F32, R + 16 + 4 * i) for i in range(2)]
        probT = [at(f"probT{i}", [P, 8, P], F32, R + 24 + 4 * i) for i in range(2)]
        oT = at("oT", [P, KC, S], F32, R + 96)
        pc = at("pc", [P, TB, H, 16], F32, R + 104)
        pcx = at("pcx", [P, TB, H, 16], F32, R + 106)
        M0 = 184.5
        causal = at("causal", [P, 2, 4, P], BF16, M0)
        identb = at("identb", [P, P], BF16, M0 + 2)
        cbias = at("cbias", [P, TB, 16], F32, M0 + 2.25)
        ckeep = at("ckeep", [P, TB, 16], F32, M0 + 2.5)
        wg = at("wg", [P, KC, 48], F32, M0 + 3)
        gateF = at("gateF", [48, S], F32, M0 + 4.5)
        gates = at("gates", [P, TB, H, 3], F32, M0 + 5.5)
        w2 = [at("cmpw2k", [P, 2, 64], F32, M0 + 6), at("cmpw2v", [P, 64], F32, M0 + 6.5)]
        mx = at("mx", [P, 16, 4], F32, M0 + 6.75)
        nm = at("nm", [P, 16, 4], F32, M0 + 7)
        sm = at("sm", [P, 16, 4], F32, M0 + 7.25)
        cf = at("cf", [P, 16, 4], F32, M0 + 7.5)
        hc = at("hc", [60, 2, P], F32, M0 + 12)
        hx = at("hx", [60, 2, P], F32, M0 + 13)
        hcT = at("hcT", [P, 2, 60], F32, M0 + 14)
        kcmp = at("kcmp", [P, G, 2, 16], F32, M0 + 14.5)
        vcmp = at("vcmp", [P, G, 64], F32, M0 + 15)
        pcT = at("pcT", [P, 2, 2, P], F32, R + 108)
        cst8 = at("cst8", [P, 4, TB * H], F32, R + 110)
        V.update({n: vec[:, 114 + 8 * i:122 + 8 * i] for i, n in enumerate(["shB1", "gmB1", "shB2", "gmB2"])})

        n_mean_ps, n_cent, n_sq, n_var_ps, n_gstd, n_grstd, n_gb_ps, n_gn, n_aff, n_bb_ps, n_bv, n_z, n_zhi, n_zlo = (
            sem(n) for n in ("mean_psum", "y_centred", "y_squared", "variance_psum", "y_std", "y_rstd",
                             "y_rstd_spread_psum", "y_normed", "y_affine", "bonus_spread_psum", "bonus_v",
                             "z_ready", "z_high", "z_low"))
        n_nrow, n_gate_ps, n_gate = sem("norm_row_loaded"), sem("gate_psum"), sem("gate_ready")
        n_xr, n_ss, n_rstd, n_x = sem("residual_loaded"), sem("row_norm"), sem("row_rnorm"), sem("residual_added")
        n_xhat, n_xT, n_full, n_hi, n_lo = (sem(n) for n in ("row_normed", "x_turned", "h_full", "h_high", "h_low"))
        n_relu, n_hhi, n_hfull, n_hlo = sem("relu_done"), sem("hidden_high"), sem("hidden_full"), sem("hidden_low")
        n_acc6 = sem("ada_sums_begun")
        n_out = sem("result_stored")
        n_kall0, n_kv, n_vt, n_kdup, n_kc, n_stk, n_qT = (sem(n) for n in (
            "keys_zeroed", "keys_copied", "values_copied_tok", "keys_doubled", "compress_input", "compress_stacked", "q_copied"))
        n_wg, n_g_ps, n_gF, n_gt_ps, n_gates = (sem(n) for n in (
            "gate_weights_loaded", "gates_psum", "gates_sigmoid", "gates_turned", "gates_ready"))
        n_w1, n_xcmp, n_hc_ps, n_hx, n_tanh, n_hc, n_hcT_ps, n_hcT, n_c_ps, n_c = (sem(n) for n in (
            "compress_weights", "compress_blocks", "compress_hidden_psum", "gelu_argument", "gelu_tanh", "gelu_done",
            "hidden_turned", "hidden_copied", "compressed_psum", "compressed"))
        n_masks = sem("attention_masks")
        n_sc_ps, n_scx, n_sce, n_pc = (sem(n) for n in ("cmp_scores", "cmp_shifted", "cmp_exp", "cmp_probs"))
        n_s_ps, n_nm, n_e, n_pr, n_pT_ps, n_pT, n_pcT, n_o_ps, n_o = (sem(n) for n in (
            "scores", "score_max", "exps", "probs", "probs_turned", "probs_copied", "cmp_probs_copied", "o_psum", "o_copied"))

        MLP_TURNS = 3
        UNITS = [(j, tb) for j in range(KC) for tb in range(TB)]
        GELU = float(np.sqrt(2 / np.pi))
        marks = {}

        def place(name, pieces):
            marks[name] = len(W_AT)
            for piece in pieces:
                (W_AT if piece[0] == "W" else A_AT).append(len(stream))
                stream.append(piece)

        def place_feed_forward(layer, beside):
            wu, wd = A["mlp_up"][layer], A["mlp_down"][layer]

            def up(g_):
                return [w_piece(wu, 512 * k, 512 * g_) for k in range(2)]

            def down(g_):
                return [w_piece(wd, 512 * g_, 512 * k) for k in range(2)]

            place(f"first{layer}", up(0))
            loop = [piece for g_ in range(1, 2 * MLP_TURNS + 1) for piece in up(g_) + down(g_ - 1)]
            place(f"loop{layer}", [x for pair_ in zip(loop, beside) for x in pair_] if beside else loop)
            place(f"last{layer}", up(7) + down(6) + down(7))

        place_feed_forward(0, [piece for part in range(6) for piece in ada_pieces(ada1, part)])
        place("kv", [w_piece(A["kv_w"], 512 * kh, 512 * b) for b in range(3) for kh in range(2)])
        place("q", [w_piece(A["nsa_wqg"][0], 512 * kh, 512 * ch) for ch in range(2) for kh in range(2)])
        place("wo", square(A["nsa_wo"][0]))
        place_feed_forward(1, [])

        def plus(n, turn, per):
            return n if turn is None else turn * per + n

        block = ctx.enter_context(nc.Block())

        def loaded(eng, p):
            eng.wait_ge(raw_in[p % RING], 16 * (p // RING + 1))

        def low_ready(eng, q):
            eng.wait_ge(s_lov, q + 1)
            eng.wait_ge(s_lop, q + 1)

        def low_half(eng, q, first):
            ks = slice(first, first + 2)
            return eng.tensor_tensor(wlo[q % 2][:, ks, :], raw[W_AT[q] % RING][:, :].rearrange(
                "p (k n) -> p k n", k=4)[:, ks, :], whi[q % 2][:, ks, :].bitcast(F32), ALU.subtract)

        @block.sync
        def _(sp):
            col = lambda a: a.rearrange("(k p) -> k p", p=P)
            for n, at_row in (("c", CC), ("rw_w0", W0), ("rw_a0", A0), ("rw_kk", KKC)):
                sp.dma_start(rows1[at_row:at_row + 8, :], col(A[n][0])).then_inc(s_rows, 16)
            sp.dma_start(rows1[KVG:KVG + 8, :], col(A["kv_norm_g"])).then_inc(s_rows, 16)
            sp.dma_start(rows1[RKC:RKC + 8, :], A["rw_rk"][0].rearrange("(j e) n -> j (e n)", e=2)).then_inc(s_rows, 16)
            sp.dma_start(rows3[:, :], col(A["ada_b"][0])).then_inc(s_rows, 16)
            used = []
            w = a = 0
            for p, (kind, src) in enumerate(stream):
                if p >= RING:
                    k, n = used[p - RING]
                    if k == "A":
                        sp.wait_ge(s_ada, n + 1)
                    else:
                        low_ready(sp, n)
                shape = dict(k=2 if kind == "A" else 4)
                sp.dma_start(raw[p % RING][:, :].rearrange("p (k n) -> p k n", **shape), src)\
                  .then_inc(raw_in[p % RING], 16)
                used.append((kind, a if kind == "A" else w))
                a, w = a + (kind == "A"), w + (kind == "W")
                if p == 7:
                    sp.dma_start(wa[:, :, :], A["rw_wa"][0].rearrange("(k p) n -> p k n", p=P)).then_inc(s_lora, 16)
                    sp.dma_start(aa[:, :, :], A["rw_aa"][0].rearrange("(k p) n -> p k n", p=P)).then_inc(s_lora, 16)
                    sp.dma_start(ga[:, :, :], A["rw_ga"][0].rearrange("(k p) n -> p k n", p=P)).then_inc(s_lora, 16)
                    sp.dma_start(wb[:, :], A["rw_wb"][0]).then_inc(s_lora, 16)
                    sp.dma_start(ab[:, :], A["rw_ab"][0]).then_inc(s_lora, 16)
                    sp.dma_start(gb0[:, :], A["rw_gb"][0, 0:P, :]).then_inc(s_lora, 16)
                    sp.dma_start(gb1[:, :], A["rw_gb"][0, P:160, :]).then_inc(s_lora, 16)
                if p == W_AT[marks["wo"]] - 1:
                    sp.wait_ge(n_kc, 1)
                    sp.wait_ge(n_gate, 4)
                    for i in range(2):
                        for e in range(2):
                            for odd in range(2):
                                sp.dma_start(stk[64 * odd:64 * odd + 64, i, e::2, 0:S - odd],
                                             kcF[64 * e:64 * e + 64, i, :, odd:S]).then_inc(n_stk, 16)
                    sp.wait_ge(n_kv, 2)
                    for e in range(2):
                        sp.dma_start(kall[64 - 64 * e:128 - 64 * e, e::2, 1 - e, :, :],
                                     kall[64 * e:64 * e + 64, e::2, e, :, :]).then_inc(n_kdup, 16)
            for b in range(TB):
                sp.wait_ge(n_x, 7 + b)
                sp.dma_start(out[0, P * b:P * b + P, :], xr[:, b, :]).then_inc(n_out, 16)
            sp.wait_ge(n_out, 16 * TB)

        @block.gpsimd
        def _(pool):
            st = Steps(pool, c_pool)
            g = nc.gpsimd
            lop, xlo_n = Tally(s_lop), Tally(s_xlo)

            def select(view, base, pattern, by, op=ALU.is_ge, fill=0.0):
                st.do(g.affine_select(out=view, in_=view, compare_op=op, fill=fill, base=base,
                                      pattern=pattern, channel_multiplier=by))

            for i in range(2):
                st.do(g.memset(gt[i][:, :], 0.0))
            st.do(g.memset(ident[:, :], 0.0))
            select(ident[:, :], 0, [[-1, P]], 1, ALU.not_equal, 1.0)
            st.do(g.memset(epsc, 1e-6))
            st.do(g.memset(gnepsc, 64e-5))
            cst = Tally(s_const)
            st.tell(g.memset(ones[:, :], 1.0), cst)
            st.do(g.memset(ind[:, :, :], 0.0))
            st.do(g.memset(bones[:, :], 0.0))
            for e in range(2):
                rows = slice(64 * e, 64 * e + 64)
                st.do(g.memset(ind[rows, :, :].rearrange("p j c -> p (j c)")[:, e:e + 18 * 7 + 1:18], 1.0))
                st.do(g.memset(bones[rows, 64 * e:64 * e + 64], 1.0))
            st.do(g.memset(indt[:, :], 1.0))
            select(indt[:, :], 0, [[1, D]], -64)
            select(indt[:, :], 63, [[-1, D]], 64)
            st.do(g.memset(tri[:, :, :], 1.0))
            for e in range(2):
                for i in range(2):
                    select(tri[64 * e:64 * e + 64, i, :], i - 1, [[1, N]], -1)
            st.do(g.memset(lm[:, :, :], 0.0))
            for level in range(6):
                b = 1 << level
                v = lm[:, level, :].rearrange("p (u a w) -> p u a w", a=2, w=b)[:, :, 1, :]
                st.do(g.memset(v, -1.0))
                select(v, 0, [[-2 * b, 64 // b], [0, b]], 1)
                select(v, b - 1, [[2 * b, 64 // b], [0, b]], -1)
            cst.next()
            g.memset(vec[:, 112:113], 0.0).then_inc(s_const, 1)
            pool.wait_ge(s_cols, 2)
            st.do(g.memset(scanmask[:, :], 1.0))
            st.tell(g.memset(scanmask[:, :].rearrange("p (u t) -> p u t", t=N)[:, :, 0:1], 0.0), cst)

            def weight_low(q):
                pool.wait_ge(s_hi, q + 1)
                st.tell(low_half(g, q, 2), lop)

            def x_low(n):
                pool.wait_ge(s_xhi, n + 1)
                st.tell(g.tensor_tensor(xlo[n % 2][:, :, :], xm[:, :, :],
                                        xhi[n % 2][:, :, :].bitcast(F32), ALU.subtract), xlo_n)

            pool.wait_ge(s_h, 2)
            for j in range(KC):
                m = MU["a"] + j
                st.do(g.tensor_scalar(xm2[:, j, :], xxF[:, j, :], pt1[:, m:m + 1], None, ALU.mult))
            st.tell(g.tensor_tensor(xm2[:, :, :], xm2[:, :, :], hF[:, :, :], ALU.add), Tally(s_mix_a))
            weight_low(0)
            weight_low(1)
            x_low(0)
            weight_low(2)
            weight_low(3)
            pool.wait_ge(s_mix, 4)
            x_low(1)
            pool.wait_ge(s_cum, 1)
            pool.wait_ge(s_t2, 2)
            kaf = Tally(s_kaf)
            for j in range(KC):
                i = g.tensor_scalar(kaF[:, j, :], aF[:, j, :], pt1[:, KAC + j:KAC + j + 1],
                                    V["omka"][:, j:j + 1], ALU.mult, ALU.add)
                st.tell(i, kaf) if j == KC - 1 else st.do(i)
            for q in range(4, 8):
                weight_low(q)
            x_low(2)
            bk0 = Tally(s_bk0)

            def zero_bk(c):
                for e in range(2):
                    i = g.memset(bk[64 * e:64 * e + 64, c, :, 1 - e, :], 0.0)
                    st.tell(i, bk0) if e else st.do(i)

            zero_bk(0)
            zero_bk(1)
            zero_bk(2)
            for q in range(8, 12):
                weight_low(q)
            pool.wait_ge(s_kaf, 1)
            pool.wait_ge(s_bonus, 1)
            st.do(g.memset(vPad[:, 0:N], 0.0))
            st.tell(g.memset(vPad[:, N + KC * S:], 0.0), bk0)
            pool.wait_ge(s_ws, 12)
            zero_bk(3)
            zeroed = Tally(s_zeroed)
            st.do(g.memset(xt_[0][:, :, :], 0.0))
            st.do(g.memset(qb[0][:, :, :, :], 0.0))
            st.do(g.memset(sv[0][:, :, :, :], 0.0))
            st.tell(g.memset(state[:, :, :], 0.0), zeroed)
            pool.wait_ge(s_bk, NCH)
            st.do(g.memset(xt_[1][:, :, :], 0.0))
            st.tell(g.memset(qb[1][:, :, :, :], 0.0), zeroed)

            ttt = [Tally(s) for s in s_tt0]
            xct = [Tally(s) for s in s_xc]

            def level_blocks(c, h, level):
                js = slice(4 * h, 4 * h + 4)
                return g.tensor_tensor(xc[:, js, :], xt_[c % 2][:, js, :],
                                       lm[:, level, :].unsqueeze(1).to_broadcast([P, 4, P]), ALU.mult)

            for what, c, h, *level in SCAN:
                js = slice(4 * h, 4 * h + 4)
                if what == "start":
                    pool.wait_ge(s_knr, 2 * c + h + 1)
                    if c:
                        pool.wait_ge(s_z_ps[h], 5 * c)
                    if c >= 2:
                        pool.wait_ge(s_u_ps, c - 1)
                    st.do(level_blocks(c, h, 0))
                    st.tell(g.tensor_tensor(tt[c % 2][:, js, :], xc[:, js, :],
                                            ident[:, :].unsqueeze(1).to_broadcast([P, 4, P]), ALU.add), ttt[h])
                    st.tell(level_blocks(c, h, 1), xct[h])
                elif what == "z" and level[0] < 4:
                    pool.wait_ge(s_z_ps[h], 5 * c + level[0] + 1)
                    st.tell(level_blocks(c, h, level[0] + 2), xct[h])

            def weight_low2(q, turn=None):
                pool.wait_ge(s_hi, plus(q + 1, turn, 8))
                st.tell(low_half(g, q, 2), lop)

            weight_low2(12)
            weight_low2(13)
            pool.wait_ge(s_y_ps, NCH)
            g.memset(zero[:, :], 0.0).then_inc(n_relu, 1)
            pool.wait_ge(s_bkt, 2 * NCH)
            pool.dma_start(xr[:, :, :], A["x"][0].rearrange("(b p) n -> p b n", p=P)).then_inc(n_xr, 16)

            def norm_row(dst, layer, which):
                pool.dma_start(dst[:, :], A["norm_g"][layer, which:which + 1, :].to_broadcast([P, D])).then_inc(n_nrow, 16)

            norm_row(nrow[0], 0, 1)
            norm_row(nrow[1], 0, 3)
            pool.wait_ge(n_grstd, 1)
            pool.wait_ge(n_gb_ps, 1)
            st.do(g.memset(acc6[:, :], 0.0))
            pool.dma_start(acc6[0:1, :], A["ada_b"][1:2, :]).then_inc(n_acc6, 16)

            def lows(name, count):
                q0 = marks[name]
                for q in range(q0, q0 + count):
                    weight_low2(q)

            def feed_forward(layer):
                lows(f"first{layer}", 3)
                q0 = marks[f"loop{layer}"]
                with pool.Fori(0, MLP_TURNS) as i:
                    st.own.enter(i, 0)
                    lop.enter(i, 8)
                    for q in range(q0 + 1, q0 + 9):
                        weight_low2(q, i)
                    st.own.leave(MLP_TURNS)
                    lop.leave(MLP_TURNS)
                for q in range(1, 6):
                    weight_low2(marks[f"last{layer}"] + q)

            pool.wait_ge(n_bv, 1)
            for l, which in ((0, 1), (1, 3)):
                norm_row(nrow_b[l], 1, which)
            weight_low2(14)
            weight_low2(15)
            feed_forward(0)
            kv0 = marks["kv"]
            weight_low2(kv0)
            weight_low2(kv0 + 1)
            pool.wait_ge(n_x, 4)
            pool.wait_ge(n_xhat, 4)
            kall0, mk = Tally(n_kall0), Tally(n_masks)
            for e in range(2):
                i = g.memset(kall[64 * e:64 * e + 64, :, 1 - e, :, :], 0.0)
                st.tell(i, kall0) if e else st.do(i)
            pool.dma_start(wg[:, :, :], A["nsa_wqg"][0, :, D:D + 48].rearrange("(k p) n -> p k n", p=P)).then_inc(n_wg, 16)
            for i, (a, b) in enumerate((("cmp_k_w1", "cmp_k_w2"), ("cmp_v_w1", "cmp_v_w2"))):
                pool.dma_start(w1[i][:, :, :], A[a].rearrange("(p r) n -> r p n", r=P)).then_inc(n_w1, 16)
                for n in range(2 - i):
                    dst = w2[1][:, :] if i else w2[0][:, n, :]
                    pool.dma_start(dst, A[b][:, :]).then_inc(n_w1, 16)
            weight_low2(kv0 + 2)
            weight_low2(kv0 + 3)
            st.do(g.memset(causal[:, :, :, :], 0.0))
            for i in range(2):
                for n in range(4):
                    if i == 0 or n % 2:
                        select(causal[:, i, n, :], 0, [[-1, P]], 1, ALU.is_ge, NEG)
            weight_low2(kv0 + 4)
            weight_low2(kv0 + 5)
            st.do(g.memset(identb[:, :], 0.0))
            select(identb[:, :], 0, [[-1, P]], 1, ALU.not_equal, 1.0)
            for t_, inside, fill in ((cbias, 0.0, NEG), (ckeep, 1.0, 0.0)):
                st.do(g.memset(t_[:, :, :], inside))
                select(t_[:, :, :], -31, [[P, TB], [-16, 16]], 1, ALU.is_ge, fill)
            st.do(g.memset(kcmp[:, :, :, :], 0.0))
            st.tell(g.memset(vcmp[:, :, :], 0.0), mk)
            lows("q", 4)
            pool.wait_ge(n_hc_ps, 1)
            st.tell(g.memset(pcT[:, :, :, :], 0.0), mk)
            lows("wo", 4)
            feed_forward(1)

        @block.scalar
        def _(act):
            col = lambda a: a.rearrange("(k p) -> k p", p=P)
            act.dma_start(rows1[0:48, :], A["rw_mu"][0].rearrange("i (k p) -> (i k) p", p=P)).then_inc(s_rows, 16)
            for n, at_row in (("rw_ka", KAC), ("rw_lng", LNG), ("rw_lnb", LNB)):
                act.dma_start(rows1[at_row:at_row + 8, :], col(A[n][0])).then_inc(s_rows, 16)
            act.dma_start(rows2[0:64, :], A["norm_g"].rearrange("l n (k p) -> (l n k) p", p=P)).then_inc(s_rows, 16)
            act.dma_start(rows2[KVB:KVB + 16, :], col(A["kv_ada_b"])).then_inc(s_rows, 16)
            act.dma_start(rows2[POSK:POSK + 16, :], A["cmp_pos_k"].rearrange("(a b) d -> a (b d)", b=2)).then_inc(s_rows, 16)
            act.dma_start(rows2[POSV:POSV + 16, :], A["cmp_pos_v"].rearrange("(a b) d -> a (b d)", b=2)).then_inc(s_rows, 16)
            act.dma_start(xt[:, :, :], A["x"][0].rearrange("(b p) n -> p b n", p=P)).then_inc(s_x, 16)
            act.wait_ge(s_const, 1)
            for i, part in enumerate((2, 5)):
                act.dma_start(gt[i][0:1, :], A["ada_b"][0:1, D * part:D * part + D]).then_inc(s_gate_bias, 16)
            st = Steps(act, c_act)
            sc = nc.scalar

            def weight_high(q):
                loaded(act, W_AT[q])
                if q >= 2:
                    act.wait_ge(s_ws, q - 1)
                sc.activation(whi[q % 2][:, :, :], raw[W_AT[q] % RING][:, :].rearrange(
                    "p (k n) -> p k n", k=4), ACT.Copy).then_inc(s_hi, 1)

            act.wait_ge(s_pt, 1)
            sc.activation(V["neg"], pt1[:, CC:CC + 8], ACT.Sigmoid).then_inc(s_sig_c, 1)
            act.wait_ge(s_x, 16)
            for b in range(TB):
                st.do(sc.activation(junk[:, :], xt[:, b, :], ACT.Square, accum_out=ss[:, b:b + 1]))
            sc.activation(std, ss, ACT.Sqrt, scale=1.0 / D, bias=epsc).then_inc(s_ss, 1)
            act.wait_ge(s_rstd, 1)
            for b in range(TB):
                sc.activation(xt[:, b, :], xt[:, b, :], ACT.Copy, scale=rstd[:, b:b + 1]).then_inc(s_xhat, 1)
            weight_high(0)
            weight_high(1)
            act.wait_ge(s_l1, 1)
            sc.activation(tw[:, :], ps[0:64, 4, 0:S], ACT.Tanh).then_inc(s_t1, 1)
            act.wait_ge(s_l1, 2)
            sc.activation(ta[:, :], ps[0:64, 5, 0:S], ACT.Copy).then_inc(s_t1, 1)
            act.wait_ge(s_l1, 3)
            sc.activation(tg0[:, :], ps[:, 6, 0:S], ACT.Sigmoid)
            sc.activation(tg1[:, :], ps[0:32, 7, 0:S], ACT.Sigmoid).then_inc(s_t1, 2)
            for i, (dst, b0, c0) in enumerate(((sgF, 0, W0), (aF, 4, A0))):
                act.wait_ge(s_l2, i + 1)
                for j in range(KC):
                    ins = sc.activation(dst[:, j, :], ps[:, b0 + j // 2, (j % 2) * S:(j % 2) * S + S],
                                        ACT.Sigmoid, bias=pt1[:, c0 + j:c0 + j + 1])
                ins.then_inc(s_t2, 1)
            act.wait_ge(s_l2, 3)
            for i in range(4):
                ins = sc.activation(gF[:, 2 * i:2 * i + 2, :].rearrange("p j t -> p (j t)"), bank(i), ACT.Copy)
            ins.then_inc(s_t2, 1)

            def x_high(n):
                act.wait_ge(s_mix, 3 + n)
                if n == 0:
                    act.wait_ge(s_l1, 3)
                if n == 1:
                    act.wait_ge(s_l2, 3)
                if n == 2:
                    act.wait_ge(s_ws, 4)
                sc.activation(xhi[n % 2][:, :, :], xm[:, :, :], ACT.Copy).then_inc(s_xhi, 1)

            def projected(n, dst):
                act.wait_ge(s_ws, 2 * n + 2)
                sc.activation(dst, bank(2 * (n % 2), 2), ACT.Copy).then_inc(s_proj_ev, 1)

            half = lambda t, h: t[:, 4 * h:4 * h + 4, :].rearrange("p j t -> p (j t)")
            x_high(0)
            act.wait_ge(s_cum, 1)
            sc.activation(sgF[:, :, :], cumF[:, :, :], ACT.Exp, scale=-DECAY).then_inc(s_dec, 1)
            act.wait_ge(s_dec, 1)
            sc.activation(cumF[:, :, :], cumF[:, :, :], ACT.Exp, scale=DECAY).then_inc(s_dec, 1)
            weight_high(2)
            projected(0, half(kF, 0))
            weight_high(3)
            x_high(1)
            weight_high(4)
            projected(1, half(kF, 1))
            act.wait_ge(s_kkraw, 1)
            sc.activation(tmpF[:, :, :], kkF[:, :, :], ACT.Square).then_inc(s_kksq, 1)
            weight_high(5)
            weight_high(6)
            act.wait_ge(s_kkn_ps, 1)
            sc.activation(s16[:, :], ps[0:H, 4, 0:S], ACT.Sqrt).then_inc(s_kkstd, 1)
            projected(2, half(tmpF, 0))
            weight_high(7)
            x_high(2)
            weight_high(8)
            projected(3, half(tmpF, 1))
            weight_high(9)
            weight_high(10)
            act.wait_ge(s_prk, 1)
            projected(4, half(vF, 0))
            weight_high(11)
            act.wait_ge(s_bonus_ps, 1)
            sc.activation(s16[:, :], ps[0:H, 4, 0:S], ACT.Copy).then_inc(s_bonus, 1)
            projected(5, half(vF, 1))

            act.wait_ge(s_zeroed, 1)
            for what, c, h, *level in SCAN:
                js, par = slice(4 * h, 4 * h + 4), c % 2
                two = bank(4, 2)
                if what == "prep":
                    if h == 0:
                        act.wait_ge(s_kr, 1)
                        if c == 1:
                            act.wait_ge(s_zeroed, 2)
                        if c >= 2:
                            act.wait_ge(s_y_ps, c - 1)
                        for e in range(2):
                            rows = slice(64 * e, 64 * e + 64)
                            ins = sc.activation(knr[par][rows, :, e, :, :].rearrange("p j a t -> p j (a t)"),
                                                krF[rows, c, :, :, :].rearrange("p j a t -> p j (a t)"), ACT.Copy)
                        ins.then_inc(s_krc, 1)
                elif what == "turn":
                    act.wait_ge(s_bkt_ps, 2 * c + h + 1)
                    v = two.rearrange("p (j e t) -> p j e t", j=4, e=2)
                    for e in range(2):
                        ins = sc.activation(bkt[par][:, js, e, :], v[:, :, e, 64 * e:64 * e + 64], ACT.Copy)
                    ins.then_inc(s_bkt, 1)
                elif what == "values":
                    act.wait_ge(s_v_ps, 2 * c + h + 1)
                    e = 1 - h
                    rows = slice(64 * (1 - e), 64 * (1 - e) + 64)
                    v = two.rearrange("p (j t) -> p j t", j=KC)[rows, :, 64 * e:64 * e + 64]
                    sc.activation(sv[par][rows, :, e, :], v, ACT.Copy)
                    sc.activation(uv[par][rows, :, e, :], v, ACT.Copy).then_inc(s_v, 1)
                elif what in ("start", "t"):
                    n = 5 * c + (level[0] + 2 if what == "t" else 1)
                    act.wait_ge(s_t_ps[h], n)
                    sc.activation(ts[:, js, :].rearrange("p j t -> p (j t)"), bank(h), ACT.Copy).then_inc(s_ts[h], 1)
                elif what == "z":
                    act.wait_ge(s_z_ps[h], 5 * c + level[0] + 1)
                    sc.activation(zs[:, js, :].rearrange("p j t -> p (j t)"), bank(h), ACT.Copy).then_inc(s_zs[h], 1)
                elif what == "w":
                    act.wait_ge(s_w_ps, c + 1)
                    sc.activation(wc[:, :, :].rearrange("p j t -> p (j t)"), bank(6), ACT.Copy).then_inc(s_w, 1)
                elif what == "u":
                    act.wait_ge(s_u_ps, c + 1)
                    for e in range(2):
                        rows = slice(64 * e, 64 * e + 64)
                        ins = sc.activation(uv[par][rows, :, e, :], ps[rows, 7, :].rearrange("p (j t) -> p j t", j=KC),
                                            ACT.Copy, scale=-1.0)
                    ins.then_inc(s_u, 1)
                elif what == "s":
                    act.wait_ge(s_st, c + 1)
                    for e in range(2):
                        rows = slice(64 * e, 64 * e + 64)
                        ins = sc.activation(sv[1 - par][rows, :, e, :], state[rows, :, :], ACT.Copy)
                    ins.then_inc(s_state_sv, 1)
                elif what == "y":
                    act.wait_ge(s_y_ps, c + 1)
                    sc.activation(yF[:, :, N * c:N * c + N], bank(7).rearrange("p (j t) -> p j t", j=KC),
                                  ACT.Copy).then_inc(s_y, 1)

            def weight_high2(q, turn=None):
                pieces = 16 if q < marks["last0"] else 8
                act.wait_ge(raw_in[W_AT[q] % RING], plus(16 * (W_AT[q] // RING + 1), turn, 16 * pieces // RING))
                act.wait_ge(s_ws, plus(q - 1, turn, 8))
                sc.activation(whi[q % 2][:, :, :], raw[W_AT[q] % RING][:, :].rearrange(
                    "p (k n) -> p k n", k=4), ACT.Copy).then_inc(s_hi, 1)

            weight_high2(12)
            weight_high2(13)
            act.wait_ge(n_cent, 1)
            sc.activation(sqF[:, :, :], yF[:, :, :], ACT.Square).then_inc(n_sq, 1)
            act.wait_ge(n_var_ps, 1)
            act.wait_ge(s_const, 2)
            sc.activation(rs16[:, :], ps[0:H, 4, 0:S], ACT.Sqrt, scale=1.0 / N, bias=gnepsc[0:H, :]).then_inc(n_gstd, 1)
            half_of = lambda t, h: t[:, 4 * h:4 * h + 4, :]
            for h in range(2):
                act.wait_ge(n_gn, h + 1)
                for j in range(4 * h, 4 * h + 4):
                    ins = sc.activation(yF[:, j, :], yF[:, j, :], ACT.Identity, scale=pt1[:, LNG + j:LNG + j + 1],
                                        bias=pt1[:, LNB + j:LNB + j + 1])
                ins.then_inc(n_aff, 1)
            for h in range(2):
                act.wait_ge(n_z, h + 1)
                sc.activation(half_of(ghi, h), half_of(zF, h), ACT.Copy).then_inc(n_zhi, 1)
            weight_high2(14)
            weight_high2(15)

            counts = dict(x=0, rstd=0, full=0)

            def row_norm(b, src):
                st.do(sc.activation(junk2[:, :], src, ACT.Square, accum_out=ss[:, b:b + 1]))
                sc.activation(std[:, b:b + 1], ss[:, b:b + 1], ACT.Sqrt, scale=1.0 / D, bias=epsc).then_inc(n_ss, 1)
                counts["rstd"] += 1

            def post_norm(q_done):
                act.wait_ge(s_ws, q_done)
                for b in range(TB):
                    row_norm(b, bank(2 * b, 2))

            def pre_norm(b0, gm, sh, hi, q):
                for b in range(TB):
                    weight_high2(q + b)
                    counts["x"] += 1
                    act.wait_ge(n_x, counts["x"])
                    row_norm(b, xr[:, b, :])
                for b in range(TB):
                    act.wait_ge(n_rstd, counts["rstd"] - 1 + b)
                    sc.activation(xn[:, b, :], xr[:, b, :], ACT.Copy, scale=rstd[:, b:b + 1]).then_inc(n_xhat, 1)
                counts["x_turned"] = counts.get("x_turned", 0) + 1
                act.wait_ge(n_xT, counts["x_turned"])
                modulated(b0, gm, sh, hi)

            def modulated(b0, gm, sh, hi):
                if counts["full"]:
                    act.wait_ge(n_lo, 2 * counts["full"])
                for j in range(4, KC):
                    ins = sc.activation(hfull[:, j, :], ps[:, b0 + j // 2, (j % 2) * S:(j % 2) * S + S], ACT.Identity,
                                        scale=V[gm][:, j:j + 1], bias=V[sh][:, j:j + 1])
                    st.do(ins) if j == KC - 1 else None
                counts["full"] += 1
                act.wait_ge(n_full, counts["full"])
                for h in range(2):
                    sc.activation(half_of(hi, h), half_of(hfull, h), ACT.Copy).then_inc(n_hi, 1)

            def feed_forward(layer):
                first, loop, last = (marks[f"{n}{layer}"] for n in ("first", "loop", "last"))

                def hidden(g_, q_done, turn=None):
                    act.wait_ge(s_ws, plus(q_done, turn, 8))
                    if g_ or layer:
                        act.wait_ge(n_hfull, plus(8 * layer + g_, turn, 2))
                    u = g_ % 2
                    sc.activation(relu[:, :, :].rearrange("p m t -> p (m t)"), bank(4 + 2 * u, 2), ACT.Relu)\
                      .then_inc(n_relu, 1)
                    act.wait_ge(n_relu, plus(8 * layer + g_ + 2, turn, 2))
                    sc.activation(hidhi[u][:, :, :], relu[:, :, :], ACT.Square).then_inc(n_hhi, 1)

                weight_high2(loop)
                hidden(0, first + 2)
                with act.Fori(0, MLP_TURNS) as i:
                    for n, g_ in enumerate((1, 2)):
                        q = loop + 4 * n
                        weight_high2(q + 1, i)
                        weight_high2(q + 2, i)
                        hidden(g_, q + 2, i)
                        weight_high2(q + 3, i)
                        weight_high2(q + 4, i)
                weight_high2(last + 1)
                weight_high2(last + 2)
                hidden(7, last + 2)
                for k in range(3, 6):
                    weight_high2(last + k)

            post_norm(16)
            pre_norm(4, "gm2", "sh2", ghi, 16)
            feed_forward(0)
            post_norm(marks["kv"])
            kv0 = marks["kv"]
            pre_norm(0, "gmkv", "shkv", ghi, kv0)
            modulated(0, "gmB1", "shB1", qhi)
            weight_high2(kv0 + 2)
            act.wait_ge(s_ws, kv0 + 2)
            sc.activation(kcF[:, :, :, :].rearrange("p a m t -> p (a m t)"), bank(4, 2), ACT.Copy).then_inc(n_kc, 1)
            weight_high2(kv0 + 3)
            act.wait_ge(n_kall0, 1)
            for br in range(2):
                weight_high2(kv0 + 4 + 2 * br)
                act.wait_ge(s_ws, kv0 + 4 + 2 * br)
                b0 = 6 if br == 0 else 4
                for e in range(2):
                    rows = slice(64 * e, 64 * e + 64)
                    ins = sc.activation(kall[rows, e::2, e, br, :], ps[rows, b0, :].rearrange("p (m t) -> p m t", m=2),
                                        ACT.Copy)
                ins.then_inc(n_kv, 1)
                ins = sc.activation(vtok[:, :, br, :], ps[:, b0 + 1, :].rearrange("p (b n) -> p b n", b=TB), ACT.Copy)
                ins.then_inc(n_vt, 1)
                weight_high2(kv0 + 5 + 2 * br)
            q0 = marks["q"]
            act.wait_ge(n_g_ps, 1)
            sc.activation(gateF[:, :], ps[0:48, 0, 0:S], ACT.Sigmoid).then_inc(n_gF, 1)

            def q_half(n):
                act.wait_ge(s_ws, q0 + 2 * n + 2)
                sc.activation(qT[:, 4 * n:4 * n + 4, :].rearrange("p j t -> p (j t)"), bank(6 - 2 * n, 2), ACT.Copy,
                              scale=N ** -0.5).then_inc(n_qT, 1)

            weight_high2(q0 + 2)
            q_half(0)
            weight_high2(q0 + 3)
            act.wait_ge(n_hx, 1)
            sc.activation(hx[:, :, :], hx[:, :, :], ACT.Tanh, scale=GELU).then_inc(n_tanh, 1)
            q_half(1)
            weight_high2(q0 + 4)
            weight_high2(q0 + 5)
            def exps(u):
                j, tb = UNITS[u]
                keys = P * (tb + 1)
                act.wait_ge(n_nm, u + 1)
                if u >= 2:
                    act.wait_ge(n_pT_ps, u - 1)
                for n in range(4):
                    src = bank(2 * (u % 2), tb + 1)[:, keys * n:keys * n + keys]
                    ins = sc.activation(prob[u % 2][:, n // 2, n % 2, 0:keys], src, ACT.Exp, bias=nm[:, u, n:n + 1],
                                        accum_out=sm[:, u, n:n + 1])
                ins.then_inc(n_e, 1)

            exps(0)
            act.wait_ge(n_scx, 1)
            sc.activation(pc[:, :, :, 0:NCMP], pcx[:, :, :, 0:NCMP], ACT.Exp).then_inc(n_sce, 1)
            for u, (j, tb) in enumerate(UNITS):
                if u + 1 < len(UNITS):
                    exps(u + 1)
                act.wait_ge(n_pT_ps, u + 1)
                if u >= 2:
                    act.wait_ge(n_o_ps, u - 1)
                sc.activation(probT[u % 2][:, 0:4 * (tb + 1), :].rearrange("p n q -> p (n q)"), bank(4, tb + 1), ACT.Copy)\
                  .then_inc(n_pT, 1)
                if u == 0:
                    act.wait_ge(n_masks, 2)
                sc.activation(pcT[0:16, u % 2, :, :].rearrange("p e q -> p (e q)"), ps[0:16, 6, 0:2 * P], ACT.Copy)\
                  .then_inc(n_pcT, 1)
            act.wait_ge(n_o, len(UNITS))
            for h in range(2):
                sc.activation(half_of(ghi, h), half_of(oT, h), ACT.Copy).then_inc(n_zhi, 1)
            weight_high2(q0 + 6)
            weight_high2(q0 + 7)
            post_norm(q0 + 8)
            pre_norm(4, "gmB2", "shB2", ghi, q0 + 8)
            feed_forward(1)
            post_norm(len(W_AT))

        @block.vector
        def _(v):
            st = Steps(v, c_dve)
            dv = nc.vector
            T = {n: Tally(s) for n, s in dict(pt=s_pt, rstd=s_rstd, h=s_h, cols=s_cols, mix=s_mix,
                 ada=s_ada, lov=s_lov, cum=s_cum, kkraw=s_kkraw, kkrs=s_kkrs, kkd=s_kkd, prk=s_prk,
                 bk=s_bk, kr=s_kr, knr=s_knr, st=s_st).items()}
            v.wait_ge(s_pt_ps, 1)
            st.tell(dv.tensor_copy(pt1[:, :], ps[:, 7, 0:120]), T["pt"])
            st.do(dv.tensor_copy(pt2[:, :], ps[:, 7, 128:240]))
            st.tell(dv.tensor_copy(pt3[:, :], ps[:, 7, 256:304]), T["pt"])
            v.wait_ge(s_sig_c, 1)
            st.do(dv.tensor_tensor(V["cs"], V["neg"], pt1[:, CC:CC + 8], ALU.mult))
            st.do(dv.tensor_scalar(V["omka"], pt1[:, KAC:KAC + 8], -1.0, 1.0, ALU.mult, ALU.add))

            def ada_piece(a, dst, i, fresh):
                loaded(v, A_AT[a])
                if a > 16 and a % 4 == 0:
                    v.wait_ge(s_cols_ps, a // 4 - 2)
                for k in range(2):
                    src, c = raw[A_AT[a] % RING][:, D * k:D * k + D], V["cs"][:, 2 * i + k:2 * i + k + 1]
                    if fresh and i == 0 and k == 0:
                        ins = dv.tensor_scalar(dst[:, :], src, c, None, ALU.mult)
                    else:
                        ins = dv.scalar_tensor_tensor(dst[:, :], src, c, dst[:, :], ALU.mult, ALU.add)
                    st.tell(ins, T["ada"]) if k else st.do(ins)

            def column(b0):
                return bank(b0, 2).rearrange("p (k n) -> p k n", k=KC)[:, :, 0]

            def shift_cols(b0, n, bias, dst):
                v.wait_ge(s_cols_ps, n)
                st.tell(dv.tensor_tensor(dst, column(b0), bias, ALU.add), T["cols"])

            def scale_cols(b0, n, bias, norm, dst):
                v.wait_ge(s_cols_ps, n)
                st.do(dv.tensor_tensor(dst, column(b0), bias, ALU.add))
                st.tell(dv.scalar_tensor_tensor(dst, dst, 1.0, norm, ALU.add, ALU.mult), T["cols"])

            for i in range(4):
                ada_piece(i, acc, i, True)
                if i == 2:
                    v.wait_ge(s_ss, 1)
                    st.tell(dv.reciprocal(rstd, std), T["rstd"])
            for i in range(4):
                ada_piece(4 + i, acc1, i, True)
            shift_cols(6, 1, pt3[:, 0:8], V["sh"])
            scale_cols(4, 2, pt3[:, 8:16], pt2[:, 0:8], V["gm"])
            v.wait_ge(s_xT, 1)
            for j in range(KC):
                ins = dv.tensor_scalar(hF[:, j, :], ps[:, j // 2, (j % 2) * S:(j % 2) * S + S],
                                       V["gm"][:, j:j + 1], V["sh"][:, j:j + 1], ALU.mult, ALU.add)
                st.tell(ins, T["h"]) if j == KC - 1 else st.do(ins)
            st.do(dv.tensor_tensor(xxF[:, :, 1:S], hF[:, :, 0:S - 1], hF[:, :, 1:S], ALU.subtract))
            st.tell(dv.tensor_scalar(xxF[:, :, 0:1], hF[:, :, 0:1], -1.0, None, ALU.mult), T["h"])

            def mix(which, dst):
                for j in range(KC):
                    m = MU[which] + j
                    ins = dv.scalar_tensor_tensor(dst[:, j, :], xxF[:, j, :], pt1[:, m:m + 1], hF[:, j, :],
                                                  ALU.mult, ALU.add)
                    st.tell(ins, T["mix"]) if j == KC - 1 else st.do(ins)

            def weight_low(q):
                v.wait_ge(s_hi, q + 1)
                st.tell(low_half(dv, q, 0), T["lov"])

            mix("w", xm)
            mix("g", xm3)
            weight_low(0)
            v.wait_ge(s_l1, 1)
            mix("k", xm)
            weight_low(1)
            v.wait_ge(s_const, 3)
            v.wait_ge(s_t2, 1)
            st.tell(dv.tensor_tensor_scan(cumF[:, :, :].rearrange("p j t -> p (j t)"), scanmask[:, :],
                                          sgF[:, :, :].rearrange("p j t -> p (j t)"), 0.0, ALU.mult, ALU.add), T["cum"])
            v.wait_ge(s_xlo, 1)
            v.wait_ge(s_xhi, 1)
            mix("r", xm)
            weight_low(2)
            weight_low(3)
            v.wait_ge(s_dec, 1)
            st.do(dv.tensor_copy(PL, sgF[:, :, :].rearrange("p j (c t) -> p c j t", t=N)[:, :, :, N - 1]))
            v.wait_ge(s_gate_bias, 32)
            for i in range(4):
                ada_piece(8 + i, gt[0], i, False)
                if i == 2:
                    weight_low(4)
            v.wait_ge(s_proj_ev, 2)
            for j in range(KC):
                ins = dv.tensor_scalar(kkF[:, j, :], kF[:, j, :], pt1[:, KKC + j:KKC + j + 1], None, ALU.mult)
                st.tell(ins, T["kkraw"]) if j == KC - 1 else st.do(ins)
            weight_low(5)
            v.wait_ge(s_kaf, 1)
            st.do(dv.tensor_tensor(kF[:, :, :], kF[:, :, :], kaF[:, :, :], ALU.mult))
            weight_low(6)
            v.wait_ge(s_xlo, 2)
            mix("v", xm)
            v.wait_ge(s_kkstd, 1)
            st.do(dv.tensor_scalar(s16[:, :], s16[:, :], 1e-12, None, ALU.max))
            st.tell(dv.reciprocal(s16[:, :], s16[:, :]), T["kkrs"])
            weight_low(7)
            for i in range(4):
                ada_piece(12 + i, gt[1], i, False)
            weight_low(8)
            weight_low(9)
            v.wait_ge(s_kkb_ps, 1)
            st.tell(dv.tensor_tensor(kkF[:, :, :].rearrange("p j t -> p (j t)"), kkF[:, :, :].rearrange(
                "p j t -> p (j t)"), bank(4, 4), ALU.mult), T["kkd"])
            st.do(dv.tensor_tensor(aF[:, :, :], aF[:, :, :], kkF[:, :, :], ALU.mult))
            v.wait_ge(s_ws, 8)
            v.wait_ge(s_proj_ev, 4)
            chunked = lambda t: t[:, :, :].rearrange("p j (c t) -> p j c t", t=N)
            krv = krF[:, :, :, :, :].rearrange("p c j a t -> p j c a t")
            for j in range(KC):
                st.do(dv.tensor_tensor(krv[:, j, :, 1, :], chunked(tmpF)[:, j], chunked(sgF)[:, j], ALU.mult))
                st.do(dv.tensor_tensor(krv[:, j, :, 0, 1:N], chunked(kkF)[:, j, :, 1:N], chunked(sgF)[:, j, :, 0:N - 1],
                                       ALU.mult))
            for c in range(NCH):
                i = dv.tensor_copy(krF[:, c, :, 0, 0:1], chunked(kkF)[:, :, c, 0:1])
                st.tell(i, T["kr"]) if c == NCH - 1 else st.do(i)
            weight_low(10)
            for j in range(KC):
                ins = dv.scalar_tensor_tensor(tmpF[:, j, :], tmpF[:, j, :], pt1[:, RKC + j:RKC + j + 1],
                                              kF[:, j, :], ALU.mult, ALU.mult)
                st.tell(ins, T["prk"]) if j == KC - 1 else st.do(ins)
            weight_low(11)
            for c in range(NCH):
                v.wait_ge(s_bk0, c + 1 + (c == 3))
                for e in range(2):
                    rows, cols = slice(64 * e, 64 * e + 64), slice(N * c, N * c + N)
                    for x, first in ((aF, e), (kF, 1 - e)):
                        ins = dv.tensor_tensor(bk[rows, c, :, e, 64 * first:64 * first + 64], x[rows, :, cols],
                                               cumF[rows, :, cols], ALU.mult)
                        st.tell(ins, T["bk"]) if (e and x is kF) else st.do(ins)

            ttt = [Tally(s) for s in s_tt]
            v.wait_ge(s_zeroed, 1)
            for what, c, h, *level in SCAN:
                js, par = slice(4 * h, 4 * h + 4), c % 2
                if what == "prep":
                    v.wait_ge(s_prep_ps, 2 * c + h + 1)
                    if c == 1 and h == 0:
                        v.wait_ge(s_zeroed, 2)
                    if c >= 2:
                        v.wait_ge(s_y_ps, c - 1)
                    pv = bank(4, 2).rearrange("p (j e a t) -> p j e a t", j=4, e=2, a=2)
                    for e in range(2):
                        own, other = slice(64 * e, 64 * e + 64), slice(64 * (1 - e), 64 * (1 - e) + 64)
                        st.do(dv.tensor_tensor(
                            knr[par][other, js, e, :, :].rearrange("p j a t -> p j (a t)"),
                            pv[other, :, e, :, :].rearrange("p j a t -> p j (a t)"),
                            tri[other, :, :].rearrange("p a t -> p (a t)").unsqueeze(1).to_broadcast([64, 4, P]),
                            ALU.mult))
                        st.do(dv.tensor_tensor(qb[par][own, js, e, :], pv[own, :, e, 1, :],
                                               tri[own, 1, :].unsqueeze(1).to_broadcast([64, 4, N]), ALU.mult))
                        ins = dv.tensor_copy(xt_[par][own, js, 64 * e:64 * e + 64], pv[own, :, e, 0, :])
                        st.tell(ins, T["knr"]) if e else st.do(ins)
                elif what == "p":
                    v.wait_ge(s_p_ps[h], 5 * c + level[0] + 1)
                    cur = tt[par][:, js, :].rearrange("p j t -> p (j t)")
                    st.tell(dv.tensor_tensor(cur, cur, bank(2 + h), ALU.add), ttt[h])
                elif what == "ada":
                    ada_piece(16 + c, acc, c % 4, True)
                elif what == "cols":
                    bias, dst, norm = ((pt3[:, 24:32], "sh2", None), (pt3[:, 32:40], "gm2", pt2[:, 16:24]),
                                       (pt2[:, KVB:KVB + 8], "shkv", None),
                                       (pt2[:, KVB + 8:KVB + 16], "gmkv", pt1[:, KVG:KVG + 8]))[c]
                    if norm is None:
                        shift_cols(4, 3 + c, bias, V[dst])
                    else:
                        scale_cols(4, 3 + c, bias, norm, V[dst])
                elif what == "s":
                    v.wait_ge(s_st_ps, c + 1)
                    flat = lambda t: t[:, :, :].rearrange("p j t -> p (j t)")
                    st.do(dv.tensor_tensor(flat(wc), bank(6), flat(state), ALU.add))
                    if c:
                        v.wait_ge(s_state_sv, c)
                    st.tell(dv.tensor_tensor(state[:, :, :], wc[:, :, :],
                                             PL[:, c, :].unsqueeze(2).to_broadcast([P, KC, N]), ALU.mult), T["st"])

            T.update({n: Tally(s) for n, s in dict(cent=n_cent, grstd=n_grstd, gn=n_gn, bv=n_bv, z=n_z, zlo=n_zlo,
                      gate=n_gate, nrstd=n_rstd, x=n_x, full=n_full, lo=n_lo, hfull=n_hfull, hlo=n_hlo).items()})
            flat = lambda t: t[:, :, :].rearrange("p j t -> p (j t)")

            def weight_low2(q, turn=None):
                v.wait_ge(s_hi, plus(q + 1, turn, 8))
                st.tell(low_half(dv, q, 0), T["lov"])

            def gate_row(n, dst, norm):
                v.wait_ge(n_gate_ps, n)
                st.tell(dv.tensor_tensor(dst[:, :], bank(6, 2), norm[:, :], ALU.mult), T["gate"])

            v.wait_ge(n_mean_ps, 1)
            st.tell(dv.scalar_tensor_tensor(flat(yF), bank(0, 4), -1.0 / N, flat(yF), ALU.mult, ALU.add), T["cent"])
            v.wait_ge(n_nrow, 32)
            gate_row(1, gt[0], nrow[0])
            v.wait_ge(n_gstd, 1)
            st.tell(dv.reciprocal(rs16[:, :], rs16[:, :]), T["grstd"])
            gate_row(2, gt[1], nrow[1])
            v.wait_ge(n_bb_ps, 1)
            st.tell(dv.tensor_tensor(flat(sqF), bank(0, 4), vPad[:, N:N + KC * S], ALU.mult), T["bv"])
            half = lambda t, h: t[:, 4 * h:4 * h + 4, :].rearrange("p j t -> p (j t)")
            v.wait_ge(n_gb_ps, 1)
            for h in range(2):
                st.tell(dv.tensor_tensor(half(yF, h), half(yF, h), bank(4 + 2 * h, 2), ALU.mult), T["gn"])
            weight_low2(12)
            weight_low2(13)

            def split_z(z, n):
                for h in range(2):
                    v.wait_ge(n_zhi, n + h + 1)
                    st.tell(dv.tensor_tensor(half(glo, h), half(z, h), half(ghi, h).bitcast(F32), ALU.subtract), T["zlo"])

            for h in range(2):
                v.wait_ge(n_aff, h + 1)
                st.do(dv.tensor_tensor(half(yF, h), half(yF, h), half(sqF, h), ALU.add))
                st.tell(dv.tensor_tensor(half(zF, h), half(yF, h), half(gF, h), ALU.mult), T["z"])
            split_z(zF, 0)
            weight_low2(14)
            weight_low2(15)

            norms = [0, 0, 0]

            def row_rnorm(b):
                norms[0] += 1
                v.wait_ge(n_ss, norms[0])
                st.tell(dv.reciprocal(rstd[:, b:b + 1], std[:, b:b + 1]), T["nrstd"])

            def post_norm(gate):
                for b in range(TB):
                    row_rnorm(b)
                    st.do(dv.scalar_tensor_tensor(pn[:, :], bank(2 * b, 2), rstd[:, b:b + 1], gate[:, :], ALU.mult, ALU.mult))
                    st.tell(dv.tensor_tensor(xr[:, b, :], xr[:, b, :], pn[:, :], ALU.add), T["x"])

            def modulated(b0, gm, sh, hi, lo):
                for j in range(4):
                    ins = dv.tensor_scalar(hfull[:, j, :], ps[:, b0 + j // 2, (j % 2) * S:(j % 2) * S + S],
                                           V[gm][:, j:j + 1], V[sh][:, j:j + 1], ALU.mult, ALU.add)
                    st.tell(ins, T["full"]) if j == 3 else st.do(ins)
                half_of = lambda t, h: t[:, 4 * h:4 * h + 4, :]
                for h in range(2):
                    norms[2] += 1
                    v.wait_ge(n_hi, norms[2])
                    st.tell(dv.tensor_tensor(half_of(lo, h), half_of(hfull, h), half_of(hi, h).bitcast(F32), ALU.subtract),
                            T["lo"])

            def pre_norm(b0, gm, sh, hi, lo, q):
                for b in range(TB):
                    row_rnorm(b)
                for b in range(2):
                    weight_low2(q + b)
                norms[1] += 1
                v.wait_ge(n_xT, norms[1])
                modulated(b0, gm, sh, hi, lo)

            def feed_forward(layer):
                first, loop, last = (marks[f"{n}{layer}"] for n in ("first", "loop", "last"))

                def hidden(g_, turn=None):
                    u = g_ % 2
                    v.wait_ge(n_relu, plus(8 * layer + g_ + 2, turn, 2))
                    st.tell(dv.tensor_tensor(hid[:, :, :], relu[:, :, :], relu[:, :, :], ALU.mult), T["hfull"])
                    v.wait_ge(n_hhi, plus(8 * layer + g_ + 1, turn, 2))
                    st.tell(dv.tensor_tensor(hidlo[u][:, :, :], hid[:, :, :], hidhi[u][:, :, :].bitcast(F32), ALU.subtract),
                            T["hlo"])

                def ada_next(t, turn):
                    a = 32 + t
                    v.wait_ge(raw_in[A_AT[a] % RING], plus(16 * (A_AT[a] // RING + 1), turn, 64))
                    for k in range(2):
                        n = 2 * (t % 4) + k
                        dst = acc6[:, bass.ds(turn * 2048 + 1024 * (t // 4), D)]
                        ins = dv.scalar_tensor_tensor(dst, raw[A_AT[a] % RING][:, D * k:D * k + D],
                                                      V["cs"][:, n:n + 1], dst, ALU.mult, ALU.add)
                        st.tell(ins, T["ada"]) if k else st.do(ins)

                weight_low2(loop)
                hidden(0)
                per_turn = dict(lov=8, hfull=2, hlo=2)
                if layer == 0:
                    v.wait_ge(n_acc6, 16)
                    per_turn["ada"] = 8
                with v.Fori(0, MLP_TURNS) as i:
                    st.own.enter(i, 0 if layer else 8)
                    for n, per in per_turn.items():
                        T[n].enter(i, per)
                    for n in range(2):
                        weight_low2(loop + 4 * n + 1, i)
                        if layer == 0:
                            ada_next(4 * n, i)
                        weight_low2(loop + 4 * n + 2, i)
                        if layer == 0:
                            ada_next(4 * n + 1, i)
                        hidden(1 + n, i)
                        weight_low2(loop + 4 * n + 3, i)
                        if layer == 0:
                            ada_next(4 * n + 2, i)
                        weight_low2(loop + 4 * n + 4, i)
                        if layer == 0:
                            ada_next(4 * n + 3, i)
                    st.own.leave(MLP_TURNS)
                    for n in per_turn:
                        T[n].leave(MLP_TURNS)
                for k in (1, 2):
                    weight_low2(last + k)
                hidden(7)
                for k in range(3, 6):
                    weight_low2(last + k)

            v.wait_ge(n_xr, 16)
            post_norm(gt[0])
            pre_norm(4, "gm2", "sh2", ghi, glo, 16)
            feed_forward(0)
            post_norm(gt[1])

            T.update({n: Tally(s_) for n, s_ in dict(gates=n_gates, xcmp=n_xcmp, hx=n_hx, hc=n_hc, hcT=n_hcT, c=n_c, scx=n_scx,
                      pc=n_pc, nm=n_nm, pr=n_pr, o=n_o).items()})
            for n, (name, norm) in enumerate((("shB1", None), ("gmB1", 32), ("shB2", None), ("gmB2", 48))):
                v.wait_ge(s_cols_ps, 7 + n)
                src = column(4 + 2 * (n % 2))
                if norm is None:
                    st.tell(dv.tensor_copy(V[name], src), T["cols"])
                else:
                    st.tell(dv.scalar_tensor_tensor(V[name], src, 1.0, pt2[:, norm:norm + 8], ALU.add, ALU.mult), T["cols"])
            v.wait_ge(n_nrow, 64)
            gate_row(3, gB[0], nrow_b[0])
            gate_row(4, gB[1], nrow_b[1])
            kv0, q0 = marks["kv"], marks["q"]
            pre_norm(0, "gmkv", "shkv", ghi, glo, kv0)
            modulated(0, "gmB1", "shB1", qhi, qlo)
            for q in range(kv0 + 2, q0 + 2):
                weight_low2(q)
            v.wait_ge(n_stk, 16 * 8)
            for i, pos in enumerate((POSK, POSV)):
                for h in range(2):
                    src = stk[:, i, :, :].rearrange("q g (n s) -> q s g n", s=16)[:, 0:16:2, :, h:h + NCMP]
                    for p in range(8):
                        a = 8 * h + p
                        ins = dv.tensor_scalar(xcmp[:, i, a, 0:60].rearrange("q (g n) -> q g n", n=NCMP), src[:, p],
                                               pt2[:, pos + a:pos + a + 1], None, ALU.add)
                        st.tell(ins, T["xcmp"]) if i and a == 15 else st.do(ins)
            v.wait_ge(n_gt_ps, 1)
            for b in range(TB):
                ins = dv.tensor_copy(gates[:, b, :, :].rearrange("p h i -> p (h i)"), ps[:, 1, P * b:P * b + 48])
                st.tell(ins, T["gates"]) if b else st.do(ins)
            v.wait_ge(n_hc_ps, 1)
            both = lambda t: t[:, :, :].rearrange("p i n -> p (i n)")
            st.do(dv.tensor_copy(both(hc), ps[0:60, 2, 0:2 * P]))
            st.do(dv.tensor_tensor(both(hx), both(hc), both(hc), ALU.mult))
            st.do(dv.tensor_scalar(both(hx), both(hx), 0.044715, 1.0, ALU.mult, ALU.add))
            st.tell(dv.tensor_tensor(both(hx), both(hx), both(hc), ALU.mult), T["hx"])
            weight_low2(q0 + 2)
            weight_low2(q0 + 3)
            v.wait_ge(n_tanh, 1)
            st.do(dv.scalar_tensor_tensor(both(hc), both(hx), 1.0, both(hc), ALU.add, ALU.mult))
            st.tell(dv.tensor_scalar(both(hc), both(hc), 0.5, None, ALU.mult), T["hc"])
            v.wait_ge(n_hcT_ps, 1)
            st.tell(dv.tensor_copy(hcT[:, :, :], ps[:, 3, 0:P].rearrange("p (i n) -> p i n", i=2)[:, :, 0:60]), T["hcT"])
            def maxima(u):
                j, tb = UNITS[u]
                v.wait_ge(n_s_ps, u + 1)
                src = bank(2 * (u % 2), tb + 1).rearrange("p (n k) -> p n k", n=4)
                st.do(dv.tensor_reduce(mx[:, u, :], src, axis=AX.X, op=ALU.max))
                st.tell(dv.tensor_scalar(nm[:, u, :], mx[:, u, :], -1.0, None, ALU.mult), T["nm"])

            maxima(0)
            v.wait_ge(n_c_ps, 1)
            v.wait_ge(n_masks, 1)
            for e in range(2):
                rows = slice(64 * e, 64 * e + 64)
                st.do(dv.tensor_copy(kcmp[rows, :, e, 0:NCMP], ps[rows, 2, 0:60].rearrange("p (g n) -> p g n", g=G)))
            st.tell(dv.tensor_copy(vcmp[0:NCMP, :, :].rearrange("p g d -> p (g d)"), ps[0:NCMP, 2, 64:64 + G * 64]), T["c"])
            weight_low2(q0 + 4)
            weight_low2(q0 + 5)

            v.wait_ge(n_sc_ps, 1)
            v.wait_ge(n_masks, 2)
            cm, cs_, cfac = (cst8[:, i, :].rearrange("p (b h) -> p b h", b=TB) for i in range(3))
            px, pe_ = pcx[:, :, :, 0:NCMP], pc[:, :, :, 0:NCMP]
            wide = lambda t: t[:, :, 0:NCMP].unsqueeze(2).to_broadcast([P, TB, H, NCMP])
            deep = lambda t: t.unsqueeze(3).to_broadcast([P, TB, H, NCMP])
            for b in range(TB):
                st.do(dv.tensor_tensor(px[:, b], ps[:, 7, 240 * b:240 * b + 240].rearrange("p (h n) -> p h n", h=H),
                                       wide(cbias)[:, b], ALU.add))
            st.do(dv.tensor_reduce(cm, px, axis=AX.X, op=ALU.max))
            for b in range(TB):
                ins = dv.tensor_tensor(px[:, b], px[:, b], deep(cm)[:, b], ALU.subtract)
                st.tell(ins, T["scx"]) if b else st.do(ins)
            maxima(1)
            v.wait_ge(n_sce, 1)
            st.do(dv.memset(pc[:, :, :, NCMP:16], 0.0))
            for b in range(TB):
                st.do(dv.tensor_tensor(pe_[:, b], pe_[:, b], wide(ckeep)[:, b], ALU.mult))
            st.do(dv.tensor_reduce(cs_, pe_, axis=AX.X, op=ALU.add))
            st.do(dv.tensor_scalar(cs_, cs_, 1e-30, None, ALU.max))
            st.do(dv.reciprocal(cs_, cs_))
            st.do(dv.tensor_tensor(cfac, cs_, gates[:, :, :, 0], ALU.mult))
            for b in range(TB):
                ins = dv.tensor_tensor(pe_[:, b], pe_[:, b], deep(cfac)[:, b], ALU.mult)
                st.tell(ins, T["pc"]) if b else st.do(ins)

            def o_copied(u):
                j, tb = UNITS[u]
                v.wait_ge(n_o_ps, u + 1)
                st.tell(dv.tensor_copy(oT[:, j, P * tb:P * tb + P], ps[:, 7, 0:P]), T["o"])

            for u, (j, tb) in enumerate(UNITS):
                v.wait_ge(n_e, u + 1)
                keys = P * (tb + 1)
                st.do(dv.reciprocal(cf[:, u, :], sm[:, u, :]))
                st.do(dv.tensor_tensor(cf[:, u, :].rearrange("p (e b) -> p e b", e=2),
                                       cf[:, u, :].rearrange("p (e b) -> p e b", e=2), gates[:, tb, 2 * j:2 * j + 2, 1:3], ALU.mult))
                p_ = prob[u % 2][:, :, :, :].rearrange("p e b k -> p (e b) k")[:, :, 0:keys]
                st.tell(dv.tensor_tensor(p_, p_, cf[:, u, :].unsqueeze(2).to_broadcast([P, 4, keys]), ALU.mult), T["pr"])
                if u:
                    o_copied(u - 1)
                if u + 2 < len(UNITS):
                    maxima(u + 2)
            o_copied(len(UNITS) - 1)
            split_z(oT, 2)
            weight_low2(q0 + 6)
            weight_low2(q0 + 7)
            post_norm(gB[0])
            pre_norm(4, "gmB2", "shB2", ghi, glo, q0 + 8)
            feed_forward(1)
            post_norm(gB[1])

        @block.tensor
        def _(pe):
            mm = nc.tensor.matmul
            tr = nc.tensor.transpose
            pe.wait_ge(s_const, 1)
            pe.wait_ge(s_rows, 16 * 15)
            tr(ps[:, 7, 0:120], rows1[:, :], ident[0:120, 0:120])
            tr(ps[:, 7, 128:240], rows2[:, :], ident[0:112, 0:112])
            tr(ps[:, 7, 256:304], rows3[:, :], ident[0:48, 0:48]).then_inc(s_pt_ps, 1)
            for b in range(TB):
                pe.wait_ge(s_xhat, b + 1)
                for j in range(KC):
                    at_ = (j % 2) * S + P * b
                    ins = tr(ps[:, j // 2, at_:at_ + P], xt[:, b, P * j:P * j + P], ident[:, :])
            ins.then_inc(s_xT, 1)

            def ada_columns(src, b0):
                for j in range(KC):
                    ins = mm(ps[:, b0 + j // 4, P * (j % 4):P * (j % 4) + P], src[:, P * j:P * j + P], ones[:, :],
                             start=True, stop=True)
                ins.then_inc(s_cols_ps, 1)

            pe.wait_ge(s_pt, 2)
            pe.wait_ge(s_ada, 4)
            ada_columns(acc, 6)
            pe.wait_ge(s_ada, 8)
            ada_columns(acc1, 4)
            pe.wait_ge(s_lora, 16 * 7)
            pe.wait_ge(s_cols, 2)
            for i, (w, x, m0, m1, b) in enumerate(((wa, xm, 0, 64, 4), (aa, xm2, 0, 64, 5), (ga, xm3, 0, P, 6),
                                                  (ga, xm3, P, 160, 7))):
                if i == 1:
                    pe.wait_ge(s_mix_a, 1)
                else:
                    pe.wait_ge(s_mix, 2 if i else 1)
                for k in range(KC):
                    ins = mm(ps[0:m1 - m0, b, 0:S], w[:, k, m0:m1], x[:, k, :], start=(k == 0), stop=(k == KC - 1))
                if i != 2:
                    ins.then_inc(s_l1, 1)

            for i, (b0, parts) in enumerate(((0, [(wb, tw)]), (4, [(ab, ta)]), (0, [(gb0, tg0), (gb1, tg1)]))):
                pe.wait_ge(s_t1, i + 1 + (i == 2))
                if i == 0:
                    pe.wait_ge(s_h, 1)
                if i == 1:
                    pe.wait_ge(s_t1, 4)
                if i == 2:
                    pe.wait_ge(s_t2, 1)
                for j in range(KC):
                    out_ = ps[:, b0 + j // 2, (j % 2) * S:(j % 2) * S + S]
                    for n, (w, x) in enumerate(parts):
                        ins = mm(out_, w[:, P * j:P * j + P], x[:, :], start=(n == 0), stop=(n == len(parts) - 1))
                ins.then_inc(s_l2, 1)

            def parts_ready(q):
                pe.wait_ge(s_hi, q + 1)
                low_ready(pe, q)

            def weights_by_x(q, m_out, hi, lo, k0, first, last):
                parts_ready(q)
                b = q % 2
                for m, out_ in enumerate(m_out):
                    for k in range(4):
                        cols = slice(P * m, P * m + P)
                        mm(out_, whi[b][:, k, cols], hi[:, k0 + k, :], start=(first and k == 0 and m % 2 == 0),
                           stop=False, skip_group_check=True)
                        mm(out_, whi[b][:, k, cols], lo[:, k0 + k, :], start=False, stop=False, skip_group_check=True)
                        ins = mm(out_, wlo[b][:, k, cols], hi[:, k0 + k, :], start=False, stop=(last and k == 3),
                                 skip_group_check=True)
                ins.then_inc(s_ws, 1)
                return ins

            def projection_half(n):
                i = n // 2
                if n % 2 == 0:
                    pe.wait_ge(s_xhi, i + 1)
                    pe.wait_ge(s_xlo, i + 1)
                if n < 2:
                    pe.wait_ge(s_t2, 3)
                else:
                    pe.wait_ge(s_proj_ev, n - 1)
                outs = [ps[:, 2 * (n % 2) + m // 2, (m % 2) * S:(m % 2) * S + S] for m in range(4)]
                for kh in range(2):
                    weights_by_x(2 * n + kh, outs, xhi[i % 2], xlo[i % 2], 4 * kh, kh == 0, kh == 1)

            projection_half(0)
            projection_half(1)
            projection_half(2)
            pe.wait_ge(s_kksq, 1)
            pe.wait_ge(s_t2, 3)
            for j in range(KC):
                ins = mm(ps[0:H, 4, 0:S], ind[:, j, :], tmpF[:, j, :], start=(j == 0), stop=(j == KC - 1))
            ins.then_inc(s_kkn_ps, 1)
            projection_half(3)
            pe.wait_ge(s_kkrs, 1)
            for j in range(KC):
                ins = mm(ps[:, 4 + j // 2, (j % 2) * S:(j % 2) * S + S], indt[:, P * j:P * j + P], s16[:, :],
                         start=True, stop=True)
            ins.then_inc(s_kkb_ps, 1)
            projection_half(4)
            pe.wait_ge(s_prk, 1)
            pe.wait_ge(s_kkd, 1)
            for j in range(KC):
                ins = mm(ps[0:H, 4, 0:S], ind[:, j, :], tmpF[:, j, :], start=(j == 0), stop=(j == KC - 1))
            ins.then_inc(s_bonus_ps, 1)
            projection_half(5)

            heads = [(j, e) for j in range(KC) for e in range(2)]
            pe.wait_ge(s_bonus, 1)
            pe.wait_ge(s_proj_ev, 6)
            pe.wait_ge(s_bk0, 5)
            for what, c, h, *level in SCAN:
                par, js = c % 2, range(4 * h, 4 * h + 4)
                mine = [(j, e) for j in js for e in range(2)]
                if what == "prep":
                    if h == 0:
                        pe.wait_ge(s_bk, c + 1)
                        pe.wait_ge(s_kr, 1)
                        if c:
                            pe.wait_ge(s_v, 2 * c)
                            pe.wait_ge(s_cols, 1 + c)
                    else:
                        pe.wait_ge(s_bkt, 2 * c + 1)
                    for n, (j, e) in enumerate(mine):
                        ins = mm(ps[:, 4 + n // 4, P * (n % 4):P * (n % 4) + P], bk[:, c, j, e, :],
                                 krF[:, c, j, :, :].rearrange("p a t -> p (a t)"), start=True, stop=True)
                    ins.then_inc(s_prep_ps, 1)
                elif what == "turn":
                    pe.wait_ge(s_knr, 2 * c + h + 1)
                    for n, (j, e) in enumerate(mine):
                        ins = tr(ps[:, 4 + n // 4, P * (n % 4):P * (n % 4) + P], bk[:, c, j, e, :], ident[:, :])
                    ins.then_inc(s_bkt_ps, 1)
                elif what == "values":
                    if h:
                        pe.wait_ge(s_v, 2 * c + 1)
                    else:
                        pe.wait_ge(s_bkt, 2 * c + 2)
                    w = c - h
                    for j in range(KC):
                        t0 = N + S * j + N * w
                        ins = tr(ps[:, 4 + j // 4, P * (j % 4):P * (j % 4) + P], vPad[:, t0:t0 + P], ident[:, :])
                    ins.then_inc(s_v_ps, 1)
                elif what == "cols":
                    pe.wait_ge(s_ada, 16 + 4 * c + 4)
                    pe.wait_ge(s_v, h)
                    ada_columns(acc, 4)
                elif what in ("start", "t"):
                    if what == "start":
                        pe.wait_ge(s_tt0[h], c + 1)
                        if c:
                            pe.wait_ge(s_zs[h], 5 * c)
                    else:
                        pe.wait_ge(s_tt[h], 5 * c + level[0] + 1)
                    for n, j in enumerate(js):
                        ins = tr(ps[:, h, P * n:P * n + P], tt[par][:, j, :], ident[:, :])
                    ins.then_inc(s_t_ps[h], 1)
                elif what == "z":
                    pe.wait_ge(s_xc[h], 5 * c + level[0] + 1)
                    pe.wait_ge(s_ts[h], 5 * c + level[0] + 1)
                    for n, j in enumerate(js):
                        ins = mm(ps[:, h, P * n:P * n + P], xc[:, j, :], ts[:, j, :], start=True, stop=True)
                    ins.then_inc(s_z_ps[h], 1)
                elif what == "p":
                    pe.wait_ge(s_zs[h], 5 * c + level[0] + 1)
                    if c or level[0]:
                        pe.wait_ge(s_tt[h], 5 * c + level[0])
                    for n, j in enumerate(js):
                        ins = mm(ps[:, 2 + h, P * n:P * n + P], zs[:, j, :], tt[par][:, j, :], start=True, stop=True)
                    ins.then_inc(s_p_ps[h], 1)
                elif what == "w":
                    pe.wait_ge(s_krc, c + 1)
                    pe.wait_ge(s_knr, 2 * c + 2)
                    pe.wait_ge(s_v, 2 * c + 2)
                    if c:
                        pe.wait_ge(s_state_sv, c)
                    for j, e in heads:
                        ins = mm(ps[64 * e:64 * e + 64, 6, N * j:N * j + N], knr[par][:, j, e, 0, :],
                                 sv[par][:, j, e, :], start=True, stop=True)
                    ins.then_inc(s_w_ps, 1)
                elif what == "u":
                    pe.wait_ge(s_w, c + 1)
                    for i in range(2):
                        pe.wait_ge(s_tt[i], 5 * c + 5)
                    if c:
                        pe.wait_ge(s_y, c)
                    for j, e in heads:
                        ins = mm(ps[64 * e:64 * e + 64, 7, N * j:N * j + N], tt[par][:, j, 64 * e:64 * e + 64],
                                 wc[:, j, :], start=True, stop=True)
                    ins.then_inc(s_u_ps, 1)
                elif what == "s":
                    pe.wait_ge(s_u, c + 1)
                    pe.wait_ge(s_bkt, 2 * c + 2)
                    for j, e in heads:
                        ins = mm(ps[64 * e:64 * e + 64, 6, N * j:N * j + N], bkt[par][:, j, e, :],
                                 uv[par][:, j, e, :], start=True, stop=True)
                    ins.then_inc(s_st_ps, 1)
                elif what == "y":
                    pe.wait_ge(s_u, c + 1)
                    for j, e in heads:
                        out_ = ps[64 * e:64 * e + 64, 7, N * j:N * j + N]
                        mm(out_, sv[par][:, j, e, :], knr[par][:, j, e, 1, :], start=True, stop=False)
                        ins = mm(out_, uv[par][:, j, e, :], qb[par][:, j, e, :], start=False, stop=True)
                    ins.then_inc(s_y_ps, 1)


            def parts_ready2(q, turn=None):
                pe.wait_ge(s_hi, plus(q + 1, turn, 8))
                pe.wait_ge(s_lov, plus(q + 1, turn, 8))
                pe.wait_ge(s_lop, plus(q + 1, turn, 8))

            def features(q, cols0, m_out, hi, lo, k0, first, turn=None):
                b = q % 2
                for m, out_ in enumerate(m_out):
                    cols = slice(cols0 + P * m, cols0 + P * m + P)
                    for k in range(4):
                        mm(out_, whi[b][:, k, cols], hi[:, k0 + k, :], start=(first and k == 0 and m % 2 == 0),
                           stop=False, skip_group_check=True)
                        mm(out_, whi[b][:, k, cols], lo[:, k0 + k, :], start=False, stop=False, skip_group_check=True)
                        ins = mm(out_, wlo[b][:, k, cols], hi[:, k0 + k, :], start=False, stop=False,
                                 skip_group_check=True)
                return ins

            def tokens(q, cols, outs, hi, lo, k0, first):
                b = q % 2
                for t, out_ in enumerate(outs):
                    rows = slice(P * t, P * t + P)
                    for k in range(4):
                        mm(out_, hi[:, k0 + k, rows], whi[b][:, k, cols], start=(first(t) and k == 0), stop=False,
                           skip_group_check=True)
                        mm(out_, lo[:, k0 + k, rows], whi[b][:, k, cols], start=False, stop=False,
                           skip_group_check=True)
                        ins = mm(out_, hi[:, k0 + k, rows], wlo[b][:, k, cols], start=False, stop=False,
                                 skip_group_check=True)
                return ins

            def halves(b0):
                return [ps[:, b0 + j // 2, (j % 2) * S:(j % 2) * S + S] for j in range(KC)]

            def gate_row(src, wait):
                if wait:
                    pe.wait_ge(n_gate, wait)
                for n in range(2):
                    ins = mm(ps[:, 6 + n, :], ones[:, :], src[:, 512 * n:512 * n + 512], start=True, stop=True)
                ins.then_inc(n_gate_ps, 1)

            pe.wait_ge(s_y, NCH)
            pe.wait_ge(s_zs[0], 5 * NCH)
            pe.wait_ge(s_zs[1], 5 * NCH)
            for j, out_ in enumerate(halves(0)):
                ins = mm(out_, bones[:, :], yF[:, j, :], start=True, stop=True)
            ins.then_inc(n_mean_ps, 1)
            gate_row(gt[0], 0)
            pe.wait_ge(n_sq, 1)
            for j in range(KC):
                ins = mm(ps[0:H, 4, 0:S], ind[:, j, :], sqF[:, j, :], start=(j == 0), stop=(j == KC - 1))
            ins.then_inc(n_var_ps, 1)
            gate_row(gt[1], 1)
            for j, out_ in enumerate(halves(0)):
                ins = mm(out_, indt[:, P * j:P * j + P], s16[:, :], start=True, stop=True)
            ins.then_inc(n_bb_ps, 1)
            pe.wait_ge(n_grstd, 1)
            pe.wait_ge(n_gate, 2)
            for j, out_ in enumerate(halves(4)):
                ins = mm(out_, indt[:, P * j:P * j + P], rs16[:, :], start=True, stop=True)
            ins.then_inc(n_gb_ps, 1)

            def out_projection(q0, n_z_):
                for ch in range(2):
                    for kh in range(2):
                        q = q0 + 2 * ch + kh
                        parts_ready2(q)
                        pe.wait_ge(n_zhi, n_z_ + kh + 1)
                        pe.wait_ge(n_zlo, n_z_ + kh + 1)
                        tokens(q, slice(0, 512), [ps[:, 2 * t + ch, :] for t in range(TB)], ghi, glo, 4 * kh,
                               lambda t: kh == 0).then_inc(s_ws, 1)

            out_projection(12, 0)

            norms = [0]

            def turned(b0):
                for b in range(TB):
                    norms[0] += 1
                    pe.wait_ge(n_xhat, norms[0])
                    for j in range(KC):
                        at_ = (j % 2) * S + P * b
                        ins = tr(ps[:, b0 + j // 2, at_:at_ + P], xn[:, b, P * j:P * j + P], ident[:, :])
                ins.then_inc(n_xT, 1)

            def h_ready(n, kh):
                pe.wait_ge(n_hi, 2 * n - 1 + kh)
                pe.wait_ge(n_lo, 2 * n - 1 + kh)

            def feed_forward(layer, n_h):
                first, loop, last = (marks[f"{n}{layer}"] for n in ("first", "loop", "last"))

                def up(g_, q, turn=None):
                    u = g_ % 2
                    if g_:
                        pe.wait_ge(n_relu, plus(8 * layer + g_, turn, 2))
                    outs = [ps[:, 4 + 2 * u + m // 2, (m % 2) * S:(m % 2) * S + S] for m in range(4)]
                    for kh in range(2):
                        if g_ == 0:
                            h_ready(n_h, kh)
                        parts_ready2(q + kh, turn)
                        features(q + kh, 0, outs, ghi, glo, 4 * kh, kh == 0).then_inc(s_ws, 1)

                def down(g_, q, turn=None):
                    u = g_ % 2
                    pe.wait_ge(n_hhi, plus(8 * layer + g_ + 1, turn, 2))
                    pe.wait_ge(n_hlo, plus(8 * layer + g_ + 1, turn, 2))
                    for ch in range(2):
                        parts_ready2(q + ch, turn)
                        tokens(q + ch, slice(0, 512), [ps[:, 2 * t + ch, :] for t in range(TB)], hidhi[u], hidlo[u], 0,
                               lambda t: False).then_inc(s_ws, 1)

                pe.wait_ge(n_x, 4 * layer + 2)
                pe.wait_ge(n_relu, 1)
                for b in range(4):
                    mm(ps[:, b, :], zero[:, :], lm[:, 0:4, :], start=True, stop=False, skip_group_check=True)
                up(0, first)
                with pe.Fori(0, MLP_TURNS) as i:
                    up(1, loop, i)
                    down(0, loop + 2, i)
                    up(2, loop + 4, i)
                    down(1, loop + 6, i)
                up(7, last)
                down(6, last + 2)
                down(7, last + 4)

            turned(4)
            feed_forward(0, 1)

            pe.wait_ge(s_ada, 56)
            pe.wait_ge(n_relu, 9)
            for n, part in enumerate((0, 1, 3, 4)):
                if n >= 2:
                    pe.wait_ge(s_cols, 5 + n)
                ada_columns(acc6[:, D * part:D * part + D], 4 + 2 * (n % 2))
            pe.wait_ge(s_cols, 10)
            gate_row(acc6[:, 2 * D:3 * D], 0)
            gate_row(acc6[:, 5 * D:6 * D], 3)
            pe.wait_ge(n_x, 4)
            turned(0)
            kv0, q0 = marks["kv"], marks["q"]
            for kh in range(2):
                h_ready(2, kh)
                parts_ready2(kv0 + kh)
                features(kv0 + kh, 0, [ps[:, 4 + m // 2, (m % 2) * S:(m % 2) * S + S] for m in range(4)],
                         ghi, glo, 4 * kh, kh == 0).then_inc(s_ws, 1)
            for br in range(2):
                b0 = 6 - 2 * br
                if br == 0:
                    pe.wait_ge(n_gate, 4)
                else:
                    pe.wait_ge(n_kc, 1)
                for kh in range(2):
                    q = kv0 + 2 + 2 * br + kh
                    parts_ready2(q)
                    features(q, 0, [ps[:, b0, S * m:S * m + S] for m in range(2)], ghi, glo, 4 * kh, kh == 0)
                    tokens(q, slice(256, 512), [ps[:, b0 + 1, S * t:S * t + S] for t in range(TB)], ghi, glo, 4 * kh,
                           lambda t: kh == 0 and t == 0).then_inc(s_ws, 1)
            pe.wait_ge(n_hi, 6)
            pe.wait_ge(n_wg, 16)
            for k in range(KC):
                ins = mm(ps[0:48, 0, 0:S], wg[:, k, :], hfull[:, k, :], start=(k == 0), stop=(k == KC - 1))
            ins.then_inc(n_g_ps, 1)
            pe.wait_ge(n_lo, 6)

            def q_half(n):
                pe.wait_ge(n_kv, n + 1)
                pe.wait_ge(n_vt, n + 1)
                for kh in range(2):
                    q = q0 + 2 * n + kh
                    parts_ready2(q)
                    features(q, 0, [ps[:, 6 - 2 * n + m // 2, (m % 2) * S:(m % 2) * S + S] for m in range(4)],
                             qhi, qlo, 4 * kh, kh == 0).then_inc(s_ws, 1)

            q_half(0)
            pe.wait_ge(n_gF, 1)
            for b in range(TB):
                ins = tr(ps[:, 1, P * b:P * b + 48], gateF[:, P * b:P * b + P], ident[0:48, 0:48])
            ins.then_inc(n_gt_ps, 1)
            pe.wait_ge(n_xcmp, 1)
            pe.wait_ge(n_w1, 16 * 5)
            for i in range(2):
                for p in range(16):
                    ins = mm(ps[0:60, 2, P * i:P * i + P], xcmp[:, i, p, 0:60], w1[i][:, p, :], start=(p == 0),
                             stop=(p == 15))
            ins.then_inc(n_hc_ps, 1)
            q_half(1)
            def scores(u):
                j, tb = UNITS[u]
                if u >= 2:
                    pe.wait_ge(n_e, u - 1)
                q_ = qT[:, j, P * tb:P * tb + P]
                for n in range(tb + 1):
                    out_ = ps[:, 2 * (u % 2) + n, :]
                    keys = kall[:, j // 2, n, :, :] if tb else kall[:, j // 2, :, :, 0:P]
                    mm(out_, q_, keys, start=True, stop=False, skip_group_check=True)
                    ins = mm(out_, identb[:, :], causal[:, tb, :, :], start=False, stop=True, skip_group_check=True)
                ins.then_inc(n_s_ps, 1)

            pe.wait_ge(n_kdup, 32)
            pe.wait_ge(n_masks, 1)
            pe.wait_ge(n_qT, 1)
            scores(0)
            pe.wait_ge(n_hc, 1)
            for i in range(2):
                ins = tr(ps[:, 3, 64 * i:64 * i + 60], hc[:, i, :], ident[0:60, 0:60])
            ins.then_inc(n_hcT_ps, 1)
            pe.wait_ge(n_hcT, 1)
            mm(ps[:, 2, 0:60], w2[0][:, :, :].rearrange("p e d -> p (e d)"), hcT[:, 0, :], start=True, stop=True)
            for g_ in range(G):
                ins = mm(ps[0:NCMP, 2, 64 + 64 * g_:128 + 64 * g_], hcT[:, 1, NCMP * g_:NCMP * g_ + NCMP], w2[1][:, :],
                         start=True, stop=True)
            ins.then_inc(n_c_ps, 1)
            pe.wait_ge(n_c, 1)
            pe.wait_ge(n_qT, 2)
            for tb in range(TB):
                for j in range(KC):
                    c0 = 2 * NCMP * (KC * tb + j)
                    ins = mm(ps[:, 7, c0:c0 + 2 * NCMP], qT[:, j, P * tb:P * tb + P], kcmp[:, j // 2, :, 0:NCMP],
                             start=True, stop=True)
            ins.then_inc(n_sc_ps, 1)

            scores(1)
            for u, (j, tb) in enumerate(UNITS):
                blocks = [(e, br, kb) for e in range(2) for br in range(2) for kb in range(tb + 1)]
                pe.wait_ge(n_pr, u + 1)
                if u:
                    pe.wait_ge(n_pT, u)
                    pe.wait_ge(n_pcT, u)
                for n, (e, br, kb) in enumerate(blocks):
                    tr(ps[:, 4 + n // 4, P * (n % 4):P * (n % 4) + P], prob[u % 2][:, e, br, P * kb:P * kb + P], ident[:, :])
                if u == 0:
                    pe.wait_ge(n_pc, 1)
                for e in range(2):
                    ins = tr(ps[0:16, 6, P * e:P * e + P], pc[:, tb, 2 * j + e, :], ident[:, :])
                ins.then_inc(n_pT_ps, 1)
                if u + 2 < len(UNITS):
                    scores(u + 2)
                pe.wait_ge(n_pT, u + 1)
                pe.wait_ge(n_pcT, u + 1)
                if u:
                    pe.wait_ge(n_o, u)
                for e in range(2):
                    out_ = ps[64 * e:64 * e + 64, 7, 0:P]
                    mm(out_, vcmp[:, j // 2, :], pcT[:, u % 2, e, :], start=True, stop=False)
                    for n, (e_, br, kb) in enumerate(blocks):
                        if e_ == e:
                            ins = mm(out_, vtok[:, kb, br, 64 * (j // 2):64 * (j // 2) + 64], probT[u % 2][:, n, :],
                                     start=False, stop=(br == 1 and kb == tb))
                ins.then_inc(n_o_ps, 1)
            out_projection(q0 + 4, 2)
            turned(4)
            feed_forward(1, 4)


def kernel(**inputs):
    import numpy as np
    import concourse.bacc as bacc
    from concourse import mybir
    from concourse.bass_utils import run_bass_kernel_spmd

    nc = bacc.Bacc("TRN2", target_bir_lowering=False, num_devices=1)
    arrays, aps = {}, {}
    for name, a in inputs.items():
        a = np.ascontiguousarray(a)
        arrays[f"in_{name}_dram"] = a
        aps[name] = nc.dram_tensor(f"in_{name}_dram", a.shape, mybir.dt.from_np(a.dtype), kind="ExternalInput").ap()
    out = nc.dram_tensor("out_0_dram", (1, S, D), mybir.dt.float32, kind="ExternalOutput").ap()
    hybrid_kernel(nc, aps, out)
    result = run_bass_kernel_spmd(nc, [arrays], core_ids=[0])
    return result.results[0]["out_0_dram"]
```
